# Optimizing a Trainium2 kernel written in Bass

```python
import math
import jax, jax.numpy as jnp
from jax import lax
import numpy as np

D_MODEL = 1024
BATCH = 1
SEQ = 512
DEPTH = 1

DN_HEADS = 8
DN_HEAD_DIM = 128
DN_WIDTH = DN_HEADS * DN_HEAD_DIM
CONV_K = 5
CHUNK = 64
MLA_HEADS = 8
Q_LORA = 512
KV_LORA = 256
NOPE_DIM = 128
ROPE_DIM = 64
V_DIM = 128
QK_DIM = NOPE_DIM + ROPE_DIM
MLA_WIDTH = MLA_HEADS * V_DIM
ROPE_THETA = 10000.0
Q_BLOCK = 128
N_EXPERTS = 16
CAPACITY_FACTOR = 2
D_EXPERT = 1024
N_BRANCHES = 2
N_MOD = 6
EPS = 1e-6

IN_SPLITS = (3 * DN_WIDTH,
             DN_WIDTH,
             2 * DN_HEADS,
             2 * DN_HEADS,
             Q_LORA,
             KV_LORA,
             ROPE_DIM,
             N_BRANCHES * D_MODEL)
N_IN = sum(IN_SPLITS)


def rms_norm(x, g):
    xf = x.astype(jnp.float32)
    y = xf * lax.rsqrt(jnp.mean(xf * xf, axis=-1, keepdims=True) + EPS)
    return (y * g.astype(jnp.float32)).astype(x.dtype)

def l2_norm(x):
    return x * lax.rsqrt(jnp.sum(x * x, axis=-1, keepdims=True) + EPS)

def apply_rope(x, cos, sin):
    x1, x2 = jnp.split(x.astype(jnp.float32), 2, axis=-1)
    return jnp.concatenate([x1 * cos - x2 * sin, x2 * cos + x1 * sin], axis=-1).astype(x.dtype)

def centred_depthwise_conv(x, w):
    ch = x.shape[-1]
    pad = (CONV_K - 1) // 2
    return lax.conv_general_dilated(x, w[:, None, :].astype(x.dtype), window_strides=(1,),
                                    padding=[(pad, pad)], dimension_numbers=('NWC', 'WIO', 'NWC'),
                                    feature_group_count=ch)

def chunk_gated_delta_rule(q, k, v, g, beta):
    b, h, s, dk = k.shape
    dv = v.shape[-1]
    nc = s // CHUNK
    q = q * (dk ** -0.5)
    qc = q.reshape(b, h, nc, CHUNK, dk)
    kc = k.reshape(b, h, nc, CHUNK, dk)
    vc = v.reshape(b, h, nc, CHUNK, dv)
    bc = beta.reshape(b, h, nc, CHUNK)
    gc = jnp.cumsum(g.reshape(b, h, nc, CHUNK), axis=-1)
    tril = jnp.tril(jnp.ones((CHUNK, CHUNK), dtype=bool))
    strict = jnp.tril(jnp.ones((CHUNK, CHUNK), dtype=bool), -1)
    diff = gc[..., :, None] - gc[..., None, :]
    decay = jnp.where(tril, jnp.exp(jnp.where(tril, diff, 0.0)), 0.0)
    k_beta = kc * bc[..., None]
    v_beta = vc * bc[..., None]
    lower = jnp.where(strict, jnp.einsum('bhnik,bhnjk->bhnij', k_beta, kc) * decay, 0.0)
    eye = jnp.eye(CHUNK, dtype=jnp.float32)
    t_inv = lax.linalg.triangular_solve(eye + lower, jnp.broadcast_to(eye, lower.shape),
                                        left_side=True, lower=True, unit_diagonal=True)
    u = t_inv @ v_beta
    w = t_inv @ (k_beta * jnp.exp(gc)[..., None])
    intra = jnp.where(tril, jnp.einsum('bhnik,bhnjk->bhnij', qc, kc) * decay, 0.0)
    q_dec = qc * jnp.exp(gc)[..., None]
    g_last = gc[..., -1]
    k_state = kc * jnp.exp(g_last[..., None] - gc)[..., None]

    def step(state, xs):
        w_i, u_i, intra_i, qd_i, ks_i, gl_i = xs
        v_new = u_i - w_i @ state
        o_i = qd_i @ state + intra_i @ v_new
        state = state * jnp.exp(gl_i)[..., None, None] + jnp.swapaxes(ks_i, -1, -2) @ v_new
        return state, o_i

    xs = tuple(jnp.moveaxis(t, 2, 0) for t in (w, u, intra, q_dec, k_state, g_last))
    state0 = jnp.zeros((b, h, dk, dv), jnp.float32)
    _, o = lax.scan(step, state0, xs)
    return jnp.moveaxis(o, 0, 2).reshape(b, h, s, dv)

def gated_deltanet_branch(qkv, z, b_in, a_in, conv_w, a_log, dt_bias, o_gain):
    bsz, s, _ = qkv.shape
    qkv = jax.nn.silu(centred_depthwise_conv(qkv, conv_w))
    q, k, v = jnp.split(qkv, 3, axis=-1)

    def heads(t):
        return t.reshape(bsz, s, DN_HEADS, DN_HEAD_DIM).transpose(0, 2, 1, 3).astype(jnp.float32)

    q, k, v = l2_norm(heads(q)), l2_norm(heads(k)), heads(v)
    beta = jax.nn.sigmoid(b_in.astype(jnp.float32)).reshape(bsz, s, 2, DN_HEADS).transpose(2, 0, 3, 1)
    a = a_in.astype(jnp.float32).reshape(bsz, s, 2, DN_HEADS)
    g = -jnp.exp(a_log.astype(jnp.float32)) * jax.nn.softplus(a + dt_bias.astype(jnp.float32))
    g = g.transpose(2, 0, 3, 1)
    o_fwd = chunk_gated_delta_rule(q, k, v, g[0], beta[0])
    flip = lambda t: jnp.flip(t, axis=2)
    o_bwd = flip(chunk_gated_delta_rule(flip(q), flip(k), flip(v), flip(g[1]), flip(beta[1])))
    o = (o_fwd + o_bwd).transpose(0, 2, 1, 3)
    zf = z.astype(jnp.float32).reshape(bsz, s, DN_HEADS, DN_HEAD_DIM)
    o = rms_norm(o, o_gain) * jax.nn.silu(zf)
    return o.reshape(bsz, s, DN_WIDTH).astype(qkv.dtype)

def mla_branch(c_q, c_kv, k_r, q_gain, w_uq, kv_gain, w_ukv, cos, sin):
    bsz, s, _ = c_q.shape
    q = (rms_norm(c_q, q_gain) @ w_uq).reshape(bsz, s, MLA_HEADS, QK_DIM)
    q = jnp.concatenate([q[..., :NOPE_DIM],
                         apply_rope(q[..., NOPE_DIM:], cos[:, :, None], sin[:, :, None])], axis=-1)
    kv = (rms_norm(c_kv, kv_gain) @ w_ukv).reshape(bsz, s, MLA_HEADS, NOPE_DIM + V_DIM)
    k_nope, v = kv[..., :NOPE_DIM], kv[..., NOPE_DIM:]
    k_rope = apply_rope(k_r, cos, sin)
    k = jnp.concatenate([k_nope, jnp.broadcast_to(k_rope[:, :, None], (bsz, s, MLA_HEADS, ROPE_DIM))], axis=-1)
    qb = (q * (QK_DIM ** -0.5)).reshape(bsz, s // Q_BLOCK, Q_BLOCK, MLA_HEADS, QK_DIM).transpose(1, 0, 2, 3, 4)

    def attend(q_blk):
        scores = jnp.einsum('bqhd,bkhd->bhqk', q_blk, k, preferred_element_type=jnp.float32)
        p = jax.nn.softmax(scores, axis=-1)
        return jnp.einsum('bhqk,bkhd->bqhd', p.astype(v.dtype), v)

    o = lax.map(attend, qb)
    return o.transpose(1, 0, 2, 3, 4).reshape(bsz, s, MLA_WIDTH)

def expert_choice_ffn(h, w_router, w_gate, w_up, w_down):
    bsz, s, d = h.shape
    cap = CAPACITY_FACTOR * s // N_EXPERTS
    aff = jax.nn.softmax((h @ w_router).astype(jnp.float32), axis=-1)
    gate, idx = lax.top_k(aff.transpose(0, 2, 1), cap)
    idx_flat = idx.reshape(bsz, N_EXPERTS * cap)
    xe = jnp.take_along_axis(h, idx_flat[..., None], axis=1).reshape(bsz, N_EXPERTS, cap, d)
    hid = jax.nn.silu(jnp.einsum('becd,edf->becf', xe, w_gate)) * jnp.einsum('becd,edf->becf', xe, w_up)
    ye = jnp.einsum('becf,efd->becd', hid, w_down) * gate[..., None].astype(h.dtype)
    out = jnp.zeros_like(h).at[jnp.arange(bsz)[:, None], idx_flat].add(ye.reshape(bsz, N_EXPERTS * cap, d))
    return out

def first_inputs(seed: int = 0) -> dict:
    key = jax.random.key(seed)
    ks = jax.random.split(key, 24)
    f32 = jnp.float32

    def nrm(k, shape, fan_in):
        return jax.random.normal(k, shape, f32) * (fan_in ** -0.5)

    def gain(k, shape):
        return 1.0 + 0.05 * jax.random.normal(k, shape, f32)

    x = jax.random.normal(ks[0], (BATCH, SEQ, D_MODEL), f32)
    c = jax.random.normal(ks[1], (BATCH, D_MODEL), f32)
    positions = (jnp.cumsum(jax.random.randint(ks[2], (BATCH, SEQ), 1, 3), axis=1) - 1).astype(jnp.int32)
    w_mod = 0.5 * nrm(ks[3], (DEPTH, D_MODEL, N_MOD * D_MODEL), D_MODEL)
    b_mod = 0.02 * jax.random.normal(ks[4], (DEPTH, N_MOD * D_MODEL), f32)
    g_mix = gain(ks[5], (DEPTH, D_MODEL))
    w_in = nrm(ks[6], (DEPTH, D_MODEL, N_IN), D_MODEL)
    conv_w = nrm(ks[7], (DEPTH, CONV_K, 3 * DN_WIDTH), CONV_K)
    a_log = jnp.log(jax.random.uniform(ks[8], (DEPTH, 2, DN_HEADS), f32, 1.0, 16.0))
    dt = jnp.exp(jax.random.uniform(ks[9], (DEPTH, 2, DN_HEADS), f32, math.log(1e-3), math.log(1e-1)))
    dt_bias = dt + jnp.log(-jnp.expm1(-dt))
    dn_o_gain = gain(ks[10], (DEPTH, DN_HEAD_DIM))
    q_gain = gain(ks[11], (DEPTH, Q_LORA))
    w_uq = nrm(ks[12], (DEPTH, Q_LORA, MLA_HEADS * QK_DIM), Q_LORA)
    kv_gain = gain(ks[13], (DEPTH, KV_LORA))
    w_ukv = nrm(ks[14], (DEPTH, KV_LORA, MLA_HEADS * (NOPE_DIM + V_DIM)), KV_LORA)
    w_o_dn = nrm(ks[15], (DEPTH, DN_WIDTH, D_MODEL), DN_WIDTH)
    w_o_mla = nrm(ks[16], (DEPTH, MLA_WIDTH, D_MODEL), MLA_WIDTH)
    w_out = nrm(ks[17], (DEPTH, D_MODEL, D_MODEL), D_MODEL)
    g_ffn = gain(ks[18], (DEPTH, D_MODEL))
    w_router = nrm(ks[19], (DEPTH, D_MODEL, N_EXPERTS), D_MODEL)
    w_gate = nrm(ks[20], (DEPTH, N_EXPERTS, D_MODEL, D_EXPERT), D_MODEL)
    w_up = nrm(ks[21], (DEPTH, N_EXPERTS, D_MODEL, D_EXPERT), D_MODEL)
    w_down = nrm(ks[22], (DEPTH, N_EXPERTS, D_EXPERT, D_MODEL), D_EXPERT)
    g_final = gain(ks[23], (D_MODEL,))
    return {'x': x, 'c': c, 'positions': positions, 'w_mod': w_mod, 'b_mod': b_mod, 'g_mix': g_mix,
            'w_in': w_in, 'conv_w': conv_w, 'a_log': a_log, 'dt_bias': dt_bias, 'dn_o_gain': dn_o_gain,
            'q_gain': q_gain, 'w_uq': w_uq, 'kv_gain': kv_gain, 'w_ukv': w_ukv, 'w_o_dn': w_o_dn,
            'w_o_mla': w_o_mla, 'w_out': w_out, 'g_ffn': g_ffn, 'w_router': w_router, 'w_gate': w_gate,
            'w_up': w_up, 'w_down': w_down, 'g_final': g_final}

def first_block(x, c, positions, w_mod, b_mod, g_mix, w_in, conv_w, a_log, dt_bias, dn_o_gain,
              q_gain, w_uq, kv_gain, w_ukv, w_o_dn, w_o_mla, w_out, g_ffn, w_router, w_gate,
              w_up, w_down, g_final):
    half = ROPE_DIM // 2
    inv_freq = ROPE_THETA ** (-jnp.arange(half, dtype=jnp.float32) / half)
    ang = positions.astype(jnp.float32)[..., None] * inv_freq
    cos, sin = jnp.cos(ang), jnp.sin(ang)
    split_at = np.cumsum(IN_SPLITS)[:-1].tolist()
    for l in range(DEPTH):
        mod = jax.nn.silu(c) @ w_mod[l] + b_mod[l]
        sh1, sc1, gt1, sh2, sc2, gt2 = jnp.split(mod[:, None, :], N_MOD, axis=-1)
        h = rms_norm(x, g_mix[l]) * (1.0 + sc1) + sh1
        proj = h @ w_in[l]
        dn_qkv, dn_z, dn_b, dn_a, c_q, c_kv, k_r, gates = jnp.split(proj, split_at, axis=-1)
        y_dn = gated_deltanet_branch(dn_qkv, dn_z, dn_b, dn_a, conv_w[l], a_log[l], dt_bias[l],
                                     dn_o_gain[l]) @ w_o_dn[l]
        y_mla = mla_branch(c_q, c_kv, k_r, q_gain[l], w_uq[l], kv_gain[l], w_ukv[l], cos, sin) @ w_o_mla[l]
        g_dn, g_mla = jnp.split(jax.nn.sigmoid(gates), N_BRANCHES, axis=-1)
        merged = g_dn * y_dn + g_mla * y_mla
        x = x + gt1 * (merged @ w_out[l])
        h = rms_norm(x, g_ffn[l]) * (1.0 + sc2) + sh2
        x = x + gt2 * expert_choice_ffn(h, w_router[l], w_gate[l], w_up[l], w_down[l])
    return rms_norm(x, g_final)


DEPTH_2 = 2

MIX_WIDTH = D_MODEL
CONV_A_WIDTH = MIX_WIDTH // 4
DIFF_WIDTH = MIX_WIDTH // 2
CONF_WIDTH = MIX_WIDTH - CONV_A_WIDTH - DIFF_WIDTH
N_DIFF_HEADS = 4
DIFF_HEAD_DIM = DIFF_WIDTH // (2 * N_DIFF_HEADS)
DIFF_V_DIM = 2 * DIFF_HEAD_DIM
SHORT_CONV_K = 3
CONF_CONV_K = 31
FFN_HIDDEN = -(-8 * D_MODEL // (3 * 256)) * 256
RMS_EPS = 1e-6
LN_EPS = 1e-5
IN_SPLITS_2 = [CONV_A_WIDTH, CONV_A_WIDTH, CONV_A_WIDTH,
             DIFF_WIDTH, DIFF_WIDTH, DIFF_WIDTH,
             2 * CONF_WIDTH]
IN_WIDTH = sum(IN_SPLITS_2)


def rmsnorm(x, g):
    xf = x.astype(jnp.float32)
    y = xf * lax.rsqrt(jnp.mean(xf * xf, axis=-1, keepdims=True) + RMS_EPS)
    return (y * g.astype(jnp.float32)).astype(x.dtype)

def layernorm(x, g, b):
    xf = x.astype(jnp.float32)
    mu = jnp.mean(xf, axis=-1, keepdims=True)
    xc = xf - mu
    y = xc * lax.rsqrt(jnp.mean(xc * xc, axis=-1, keepdims=True) + LN_EPS)
    return (y * g.astype(jnp.float32) + b.astype(jnp.float32)).astype(x.dtype)

def causal_depthwise_conv(x, w):
    k, c = w.shape
    return lax.conv_general_dilated(
        x, w.astype(x.dtype)[:, None, :], window_strides=(1,), padding=((k - 1, 0),),
        dimension_numbers=("NWC", "WIO", "NWC"), feature_group_count=c)

def rope_tables(positions):
    inv_freq = 1.0 / (ROPE_THETA ** (jnp.arange(0, DIFF_HEAD_DIM, 2, dtype=jnp.float32) / DIFF_HEAD_DIM))
    ang = positions.astype(jnp.float32)[..., None] * inv_freq
    return jnp.cos(ang)[:, :, None, None, :], jnp.sin(ang)[:, :, None, None, :]

def apply_rope_2(x, cos, sin):
    xf = x.astype(jnp.float32)
    x1, x2 = jnp.split(xf, 2, axis=-1)
    out = jnp.concatenate([x1 * cos - x2 * sin, x2 * cos + x1 * sin], axis=-1)
    return out.astype(x.dtype)

def diff_attention(q, k, v, lam):
    b, s, _, h, d = q.shape
    nb = s // Q_BLOCK
    qb = q.reshape(b, nb, Q_BLOCK, 2, h, d).transpose(1, 0, 2, 3, 4, 5)
    key_idx = jnp.arange(s)
    scale = d ** -0.5

    def block(args):
        i, qi = args
        sc = jnp.einsum("bqmhd,bkmhd->bmhqk", qi, k,
                        preferred_element_type=jnp.float32) * scale
        q_idx = i * Q_BLOCK + jnp.arange(Q_BLOCK)
        mask = key_idx[None, :] <= q_idx[:, None]
        p = jax.nn.softmax(jnp.where(mask, sc, -jnp.inf), axis=-1)
        a = p[:, 0] - lam * p[:, 1]
        return jnp.einsum("bhqk,bkhe->bqhe", a.astype(v.dtype), v)

    out = lax.map(block, (jnp.arange(nb), qb))
    return out.transpose(1, 0, 2, 3, 4).reshape(b, s, h, DIFF_V_DIM)

def mixing_layer(h, cos, sin, w_in, short_conv_w, glu_b, conf_dw_w, conf_dw_b,
                 conf_ln_g, conf_ln_b, lam_q1, lam_k1, lam_q2, lam_k2, diff_subln_g,
                 w_out, lam_init):
    b, s, _ = h.shape
    u = jnp.einsum("bsd,de->bse", h, w_in)
    offs = np.cumsum(IN_SPLITS_2)[:-1].tolist()
    a_b, a_c, a_x, q, k, v, c_in = jnp.split(u, offs, axis=-1)

    y_a = a_b * causal_depthwise_conv(a_c * a_x, short_conv_w)

    q = apply_rope_2(q.reshape(b, s, 2, N_DIFF_HEADS, DIFF_HEAD_DIM), cos, sin)
    k = apply_rope_2(k.reshape(b, s, 2, N_DIFF_HEADS, DIFF_HEAD_DIM), cos, sin)
    v = v.reshape(b, s, N_DIFF_HEADS, DIFF_V_DIM)
    lam = (jnp.exp(jnp.sum(lam_q1.astype(jnp.float32) * lam_k1.astype(jnp.float32)))
           - jnp.exp(jnp.sum(lam_q2.astype(jnp.float32) * lam_k2.astype(jnp.float32)))
           + lam_init)
    o = diff_attention(q, k, v, lam)
    o = rmsnorm(o, diff_subln_g) * (1.0 - lam_init)
    y_b = o.reshape(b, s, DIFF_WIDTH)

    c = c_in + glu_b
    c = c[..., :CONF_WIDTH] * jax.nn.sigmoid(c[..., CONF_WIDTH:])
    c = causal_depthwise_conv(c, conf_dw_w) + conf_dw_b
    y_c = jax.nn.silu(layernorm(c, conf_ln_g, conf_ln_b))

    y = jnp.concatenate([y_a, y_b, y_c], axis=-1)
    return jnp.einsum("bse,ed->bsd", y, w_out)

def swiglu(h, w_gate, w_up, w_down):
    g = jnp.einsum("bsd,df->bsf", h, w_gate)
    u = jnp.einsum("bsd,df->bsf", h, w_up)
    return jnp.einsum("bsf,fd->bsd", jax.nn.silu(g) * u, w_down)

def second_inputs(seed: int = 0) -> dict:
    key = jax.random.key(seed)
    ks = iter(jax.random.split(key, 32))
    f32 = jnp.float32

    def nrm(shape, scale):
        return jax.random.normal(next(ks), shape, f32) * scale

    x = jax.random.normal(next(ks), (BATCH, SEQ, D_MODEL), f32)
    offsets = jax.random.randint(next(ks), (BATCH, 1), 0, 1024, dtype=jnp.int32)
    positions = offsets + jnp.arange(SEQ, dtype=jnp.int32)[None, :]
    return {
        "x": x,
        "positions": positions,
        "mix_norm_g": 1.0 + nrm((DEPTH_2, D_MODEL), 0.02),
        "w_in": nrm((DEPTH_2, D_MODEL, IN_WIDTH), D_MODEL ** -0.5),
        "short_conv_w": nrm((DEPTH_2, SHORT_CONV_K, CONV_A_WIDTH), SHORT_CONV_K ** -0.5),
        "glu_b": nrm((DEPTH_2, 2 * CONF_WIDTH), 0.02),
        "conf_dw_w": nrm((DEPTH_2, CONF_CONV_K, CONF_WIDTH), CONF_CONV_K ** -0.5),
        "conf_dw_b": nrm((DEPTH_2, CONF_WIDTH), 0.02),
        "conf_ln_g": 1.0 + nrm((DEPTH_2, CONF_WIDTH), 0.02),
        "conf_ln_b": nrm((DEPTH_2, CONF_WIDTH), 0.02),
        "lam_q1": nrm((DEPTH_2, DIFF_HEAD_DIM), 0.1),
        "lam_k1": nrm((DEPTH_2, DIFF_HEAD_DIM), 0.1),
        "lam_q2": nrm((DEPTH_2, DIFF_HEAD_DIM), 0.1),
        "lam_k2": nrm((DEPTH_2, DIFF_HEAD_DIM), 0.1),
        "diff_subln_g": 1.0 + nrm((DEPTH_2, DIFF_V_DIM), 0.02),
        "w_out": nrm((DEPTH_2, MIX_WIDTH, D_MODEL), MIX_WIDTH ** -0.5),
        "ffn_norm_g": 1.0 + nrm((DEPTH_2, D_MODEL), 0.02),
        "w_gate": nrm((DEPTH_2, D_MODEL, FFN_HIDDEN), D_MODEL ** -0.5),
        "w_up": nrm((DEPTH_2, D_MODEL, FFN_HIDDEN), D_MODEL ** -0.5),
        "w_down": nrm((DEPTH_2, FFN_HIDDEN, D_MODEL), FFN_HIDDEN ** -0.5),
        "final_norm_g": 1.0 + nrm((D_MODEL,), 0.02),
    }

def second_block(x, positions, mix_norm_g, w_in, short_conv_w, glu_b, conf_dw_w, conf_dw_b,
              conf_ln_g, conf_ln_b, lam_q1, lam_k1, lam_q2, lam_k2, diff_subln_g, w_out,
              ffn_norm_g, w_gate, w_up, w_down, final_norm_g):
    cos, sin = rope_tables(positions)
    for l in range(DEPTH_2):
        lam_init = 0.8 - 0.6 * math.exp(-0.3 * l)
        h = rmsnorm(x, mix_norm_g[l])
        x = x + mixing_layer(h, cos, sin, w_in[l], short_conv_w[l], glu_b[l], conf_dw_w[l],
                             conf_dw_b[l], conf_ln_g[l], conf_ln_b[l], lam_q1[l], lam_k1[l],
                             lam_q2[l], lam_k2[l], diff_subln_g[l], w_out[l], lam_init)
        h = rmsnorm(x, ffn_norm_g[l])
        x = x + swiglu(h, w_gate[l], w_up[l], w_down[l])
    return rmsnorm(x, final_norm_g)


def setup_inputs(seed=0):
    out = dict(first_inputs(seed))
    for name, value in second_inputs(seed + 1).items():
        if name != "x":
            out[name + "_2"] = value
    return out


def reference(
    x, c, positions, w_mod, b_mod, g_mix, w_in, conv_w, a_log, dt_bias, dn_o_gain, q_gain, w_uq,
    kv_gain, w_ukv, w_o_dn, w_o_mla, w_out, g_ffn, w_router, w_gate, w_up, w_down, g_final,
    positions_2, mix_norm_g_2, w_in_2, short_conv_w_2, glu_b_2, conf_dw_w_2, conf_dw_b_2,
    conf_ln_g_2, conf_ln_b_2, lam_q1_2, lam_k1_2, lam_q2_2, lam_k2_2, diff_subln_g_2, w_out_2,
    ffn_norm_g_2, w_gate_2, w_up_2, w_down_2, final_norm_g_2,
):
    x = first_block(
        x, c, positions, w_mod, b_mod, g_mix, w_in, conv_w, a_log, dt_bias, dn_o_gain, q_gain,
        w_uq, kv_gain, w_ukv, w_o_dn, w_o_mla, w_out, g_ffn, w_router, w_gate, w_up, w_down,
        g_final,
    )
    return second_block(
        x, positions_2, mix_norm_g_2, w_in_2, short_conv_w_2, glu_b_2, conf_dw_w_2, conf_dw_b_2,
        conf_ln_g_2, conf_ln_b_2, lam_q1_2, lam_k1_2, lam_q2_2, lam_k2_2, diff_subln_g_2,
        w_out_2, ffn_norm_g_2, w_gate_2, w_up_2, w_down_2, final_norm_g_2,
    )


_drawn_inputs = setup_inputs


def setup_inputs(seed=0):
    import zlib

    import numpy as np

    out = dict(_drawn_inputs(seed))
    spreads = {}
    factors = {'g_mix': 3.314,
     'dn_o_gain': 3.682,
     'q_gain': 8.0,
     'kv_gain': 4.433,
     'g_ffn': 3.352,
     'glu_b_2': 6.726,
     'conf_dw_b_2': 3.529,
     'conf_ln_g_2': 6.58,
     'conf_ln_b_2': 7.772,
     'lam_k1_2': 4.737,
     'lam_k2_2': 8.0,
     'diff_subln_g_2': 4.528,
     'ffn_norm_g_2': 3.172,
     'final_norm_g_2': 2.824}
    for name, (base, spread) in spreads.items():
        noise = np.random.default_rng([zlib.crc32(name.encode()), seed]).standard_normal(out[name].shape)
        drawn = base * np.exp(spread * noise) if base else spread * noise
        out[name] = __import__('jax').numpy.asarray(drawn.astype(out[name].dtype))
    for name, factor in factors.items():
        out[name] = (out[name] * factor).astype(out[name].dtype)
    return out
```

```python
from contextlib import ExitStack

import numpy as np

import concourse.bass as bass
from concourse import mybir

F32 = mybir.dt.float32
I32 = mybir.dt.int32
F32R = mybir.dt.float32r
ALU = mybir.AluOpType
ACT = mybir.ActivationFunctionType
AX_X = mybir.AxisListType.X

P = 128
SEQ, DM = 512, 1024
TT = SEQ // P
KD = DM // P
EPS, LN_EPS = 1e-6, 1e-5
HEADS, HD = 8, 128
CONV_K = 5
NOPE, ROPE, VD = 128, 64, 128
QK = NOPE + ROPE
Q_LORA, KV_LORA = 512, 256
EXPERTS, CAP = 16, 64
PAIRS = EXPERTS // 2
LAYERS = 2
FB = 2816 // P
CONF_K = 31
BIG = 30000.0
MAGIC = 12582912.0
TWO_PI_HI = 6.28125
TWO_PI_MID = float(np.float32(2 * np.pi - 6.28125))
TWO_PI_LO = float(2 * np.pi - 6.28125 - np.float32(2 * np.pi - 6.28125))
PI_IN = 3.1415925

RING = 8
RAW = 4

N_MOD1 = 0
N_LATENT = N_MOD1 + 8
N_MOD2 = N_LATENT + 3
N_MERGE = N_MOD2 + 16
N_OUT = N_MERGE + 16
N_EXPERT = N_OUT + 4
PER_PAIR, PER_LAYER = 24, 48
N_LAYER = N_EXPERT + PAIRS * PER_PAIR
M_IN, M_OUT, M_UP = 0, 11, 15
M_DOWN = M_UP + FB

C_B, C_CQ, C_CKV, C_KR, C_GATES = 4096, 4128, 4640, 4896, 4960

R_C, R_BMOD, R_GMIX, R_GFFN, R_QG, R_KVG, R_OG, R_A = 0, 8, 56, 64, 72, 76, 78, 79
L_MIX, L_FFN, L_GLU, L_DWB, L_LNG, L_LNB, L_SC, L_SUB, L_DW, L_ROWS = 0, 8, 16, 20, 22, 24, 26, 32, 33, 95


def build(nc, A, out):
    ctx = ExitStack()
    sems = {}

    def sem(name):
        if name not in sems:
            sems[name] = ctx.enter_context(nc.semaphore(name))
        return sems[name]

    with ctx:
        base = nc.sbuf_base + (-nc.sbuf_base) % 64
        top = nc.sbuf_usable_end

        def at(name, offset, shape, dt=F32):
            return nc.alloc_sbuf_tensor_at(name, shape, dt, offset=base + offset)

        class Region:

            def __init__(self, start, end):
                self.pos, self.end = start, end

            def __call__(self, name, shape, dt=F32):
                t = at(name, self.pos, shape, dt)
                self.pos += 4 * int(np.prod(shape[1:]))
                self.pos += (-self.pos) % 32
                assert self.pos <= self.end, (name, self.pos, self.end)
                return t

        everything = Region(0, (top - base) // 64 * 64)
        ring = [everything(f"ring{i}", [P, 2048]) for i in range(RING)]
        x = everything("x", [P, TT, DM])
        HT_AT = everything.pos
        hT = everything("hT", [P, KD, SEQ])
        XN_AT = everything.pos
        xn = everything("xn", [P, TT, DM])
        XN_END = everything.pos
        ident = everything("ident", [P, P])
        cols_a = everything("cols_a", [P, R_A])
        cols_l = everything("cols_l", [P, L_ROWS])
        mod_sh1 = everything("mod_sh1", [P, KD])
        mod_g1 = everything("mod_g1", [P, KD])
        mod_sh2 = everything("mod_sh2", [P, KD])
        mod_g2 = everything("mod_g2", [P, KD])
        silu_c = everything("silu_c", [P, KD])
        gt2_b = everything("gt2_b", [P, DM])
        w_router = everything("w_router", [P, KD, EXPERTS])
        small = everything("small", [P, TT, 96])
        cos = everything("cos", [P, 8, 32])
        sin = everything("sin", [P, 8, 32])
        eps_col = everything("eps_col", [P, 2])
        ss = everything("ss", [P, 16])
        rms = everything("rms", [P, 16])
        rstd = everything("rstd", [P, 16])
        ARENA, ARENA_END = everything.pos, everything.end

        bank = [ctx.enter_context(nc.psum_tensor(f"bank{i}", [P, 512], F32)) for i in range(8)]

        r = Region(ARENA, ARENA_END)
        oT_dn = r("oT_dn", [P, HEADS, SEQ])
        HEADW_AT = r.pos
        head_w = r("head_w", [P, KD, 512])
        conv_out = r("conv_out", [P, 3, SEQ])
        solve_T = at("solve_T", r.pos - 6144, [P, 2, SEQ])
        o_tok = at("o_tok", r.pos - 2048, [P, TT, P])
        k_tok = r("k_tok", [P, TT, P])
        v_tok = r("v_tok", [P, TT, P])
        solve_TT = r("solve_TT", [P, 2, SEQ])
        q_tok = at("q_tok", r.pos - 4096, [P, TT, P])
        z_silu = r("z_silu", [P, TT, P])
        qnT = r("qnT", [P, SEQ])
        knT = r("knT", [P, SEQ])
        solve_N = r("solve_N", [P, 2, SEQ])
        g_wide = at("g_wide", r.pos - 4096, [P, TT, 2, P])
        solve_C = r("solve_C", [P, 2, TT, P])
        w_small = at("w_small", r.pos - 4096, [P, KD, 96])
        k_beta = r("k_beta", [P, 2, TT, P])
        wT = at("wT", r.pos - 4096, [P, 2, SEQ])
        v_beta = r("v_beta", [P, 2, TT, P])
        u = at("u", r.pos - 4096, [P, 2, TT, P])
        q_decT = r("q_decT", [P, 2, SEQ])
        v_new = r("v_new", [P, 2, P])
        state = r("state", [P, 2, P])
        tri = r("tri", [P, 2, P])
        chunk_ones = r("chunk_ones", [P, P])
        min_mask = r("min_mask", [P, 2, P])
        max_mask = r("max_mask", [P, 2, P])
        level_mask = r("level_mask", [P, 6, P])
        cols_b = r("cols_b", [P, CONV_K * 24])
        conv_col = r("conv_col", [P, CONV_K, 3])
        col_q = r("col_q", [P, 5, TT * 2, HEADS])
        head_q = r("head_q", [P, 5, TT * 2])
        xr = Region(XN_AT, XN_END)
        e_T = xr("e_T", [P, 2, TT, P])
        e_L = xr("e_L", [P, 2, TT, P])
        e_row = xr("e_row", [P, 2, SEQ])
        k_state = xr("k_state", [P, 2, TT, P])
        sr = Region(HEADW_AT + 16384, ARENA_END)
        rows_a = sr("rows_a", [R_A, P])
        rows_b = sr("rows_b", [CONV_K * 24, P])
        pos_i = sr("pos_i", [P, 8], I32)
        pos_f = sr("pos_f", [P, 8])
        inv_freq = sr("inv_freq", [P, 32])
        ang = sr("ang", [P, 8, 32])
        turns = sr("turns", [P, 8, 32])
        a_log_b = sr("a_log_b", [P, 16])
        dt_b = sr("dt_b", [P, 16])
        sp_a = sr("sp_a", [P, TT, 16])
        sp_b = sr("sp_b", [P, TT, 16])
        level_blk = sr("level_blk", [P, 7, P])
        assert sr.pos <= HEADW_AT + 16384 + 6144 + 4096 + 4096 + 2048

        r = Region(HEADW_AT, ARENA_END)
        mla_wq = r("mla_wq", [P, 4, 2 * QK])
        mla_wkv = r("mla_wkv", [P, 2, 512])
        oT_mla = r("oT_mla", [P, HEADS, SEQ])
        MERGE_AT = r.pos
        cqT = r("cqT", [P, 4, SEQ])
        ckvT = r("ckvT", [P, 2, SEQ])
        krT = r("krT", [P, SEQ])
        kr_tok = r("kr_tok", [P, TT, P])
        qT = r("qT", [P, 2, SEQ])
        kT = r("kT", [P, 2, SEQ])
        qr_tok = r("qr_tok", [P, TT, 2, 64])
        qrT = r("qrT", [P, SEQ])
        v_mla = r("v_mla", [P, TT, 256])
        probs = r("probs", [P, 2, SEQ])
        rope_t = r("rope_t", [P, 2, 256])
        nmax = r("nmax", [P, 2])
        psums = r("psums", [P, 2])
        pinv = r("pinv", [P, 2])
        pT = at("pT", XN_AT, [P, 2, TT, SEQ])
        cqn = at("cqn", XN_AT, [P, TT, 512])
        ckvn = at("ckvn", XN_AT + 8192, [P, TT, 256])
        silu_cb = at("silu_cb", XN_AT, [P, KD, P])

        r = Region(MERGE_AT, ARENA_END)
        mT = r("mT", [P, KD, SEQ])
        sig = r("sig", [P, 2, 2, SEQ])
        part = r("part", [P, 2, 2, SEQ])
        upd = r("upd", [P, 256])
        gt1_b = r("gt1_b", [P, DM])

        r = Region(ARENA, ARENA_END - 8192)
        onehot = r("onehot", [P, TT, 9 * P])
        YE_AT = r.pos
        ye = r("ye", [P, PAIRS, DM])
        xeT = r("xeT", [P, KD, P])
        hid = r("hid", [P, DM])
        hidT = r("hidT", [P, KD, P])
        slot_tok = r("slot_tok", [P, TT, EXPERTS])
        iota64 = r("iota64", [P, 64])
        iota_p = r("iota_p", [P, 1])
        scat = at("scat", HT_AT, [P, PAIRS, SEQ])
        upd2 = r("upd2", [P, 512])
        r = Region(YE_AT, ARENA_END - 8192)
        aff = r("aff", [P, TT, EXPERTS])
        amax = r("amax", [P, TT])
        asum = r("asum", [P, TT])
        affT = r("affT", [EXPERTS, SEQ])
        work = r("work", [EXPERTS, 2, SEQ])
        zeros16 = r("zeros16", [EXPERTS, SEQ])
        slotT = r("slotT", [EXPERTS, SEQ])
        top8 = r("top8", [EXPERTS, 8, 8])
        pair_sel = r("pair_sel", [EXPERTS, PAIRS, P])
        gate_b = r("gate_b", [P, 2, SEQ])

        r = Region(ARENA, ARENA_END - 8192)
        ffn_hT = r("ffn_hT", [P, FB, SEQ])
        ffn_sg = r("ffn_sg", [P, 4, SEQ])
        gfin_b = at("gfin_b", ARENA_END - 8192, [P, DM])
        gfin2_b = at("gfin2_b", ARENA_END - 4096, [P, DM])
        rows_l = r("rows_l", [L_ROWS, P])
        lam_in = r("lam_in", [P, 4, 64])
        lam_s = r("lam_s", [P, 4])
        lam_i = r("lam_i", [P, 2])
        lam_c = r("lam_c", [P, LAYERS, 2])
        lam_p = r("lam_p", [P, 2, 64])
        causal = r("causal", [P, P])
        ones = r("ones", [P, P])
        upd3 = r("upd3", [P, 2])
        ln_rs = r("ln_rs", [P, SEQ])
        conv_acc = r("conv_acc", [P, 2, SEQ])
        AFTER_FFN = r.pos
        hT_hi = at("hT_hi", HT_AT, [P, KD, SEQ], F32R)
        yT_hi = at("yT_hi", XN_AT, [P, KD, SEQ], F32R)
        ffn_hi = at("ffn_hi", XN_AT, [P, 2, 2, SEQ], F32R)
        ffn_lo = at("ffn_lo", XN_AT + 8192, [P, 2, 2, SEQ], F32R)
        raw = [ring[(N_LAYER + i) % RING] for i in range(RAW)]
        w_hi, w_lo = [], []
        for i in range(2):
            slot = (N_LAYER + RAW + 2 * i) % RING
            w_hi.append(at(f"w_hi{i}", slot * 8192, [P, 2048], F32R))
            w_lo.append(at(f"w_lo{i}", (slot + 1) * 8192, [P, 2048], F32R))
        r = Region(ARENA, ARENA + 4 * FB * SEQ)
        glu = r("glu", [P, 2, 30 + SEQ])
        conf = r("conf", [P, 2, SEQ])
        prod = r("prod", [P, 2, 2 + SEQ])
        q2T = r("q2T", [P, 4, SEQ])
        k2T = r("k2T", [P, 4, SEQ])
        v2 = r("v2", [P, TT, 512])
        aT = r("aT", [P, 2, TT, P])
        o2 = at("o2", HT_AT + 8192, [P, TT, 4, P])
        rot = [at(f"rot{i}", XN_AT + 4096 * (i + 1) if i < 3 else ARENA + 4 * FB * SEQ, [P, 2, 512]) for i in range(4)]
        r = Region(AFTER_FFN, ARENA_END - 8192)
        PARTS_AT = r.pos
        hT_lo = r("hT_lo", [P, KD, SEQ], F32R)
        yT_lo = at("yT_lo", PARTS_AT, [P, KD, SEQ], F32R)
        rope_2 = at("rope_2", ARENA + 4 * FB * SEQ + 4096, [P, 2, 256])
        p2 = at("p2", HT_AT, [P, 4, SEQ])
        sig2 = at("sig2", ARENA + 4 * FB * SEQ + 4096, [P, 2, SEQ])
        nmax2 = r("nmax2", [P, 4])
        psum2 = r("psum2", [P, 4])
        pinv2 = r("pinv2", [P, 4])

        landed = [sem(f"weights_landed_{i}") for i in range(RING)]
        chunk_used = sem("chunk_used")
        raw_landed = [sem(f"raw_landed_{i}") for i in range(RAW)]
        hi_ready, lo_ready, parts_used = sem("hi_ready"), sem("lo_ready"), sem("parts_used")
        ONCE = {
            "vector_steps": (
                "eps_ready", "cols_ready", "angles_ready", "mod1_cols", "sp_in", "g_ready", "gc_ready",
                "latent_normed", "kr_ready", "silu_cb_ready", "mod2_cols", "amax_ready", "aff_ready", "slotT_ready",
                "onehot_ready", "x_first"
            ),
            "tensor_steps": (
                "rows_turned", "mod1_done", "small_done", "gc_done", "latent_done", "kr_done", "mod2_done",
                "router_done", "aff_turned", "slot_turned"
            ),
            "scalar_steps": (
                "silu_c_ready", "rope_ready", "small_ready", "sp_ready", "gc_exp", "latent_rms", "krT_ready",
                "aff_exp", "first_rms", "last_rms"
            ),
            "pool_steps": (
                "ident_ready", "masks_ready", "route_consts", "block2_consts"
            ),
        }
        step = {name: sem(engine) for engine, names in ONCE.items() for name in names}
        step_count = {name: i + 1 for names in ONCE.values() for i, name in enumerate(names)}

        def reached(eng, name):
            eng.wait_ge(step[name], step_count[name])

        EACH_TURN = {
            "head_vector": (
                "head_q_ready", "g_wide_ready", "q_tok_ready", "k_tok_ready", "o_sum", "o_ready",
            ),
            "head_tensor": (
                "z_done", "kk_done", "kq_done", "oT_done",
            ),
            "head_scalar": (
                "z_ready", "len_ready", "v_tok_ready", "o_fwd_ready", "o_rms",
            ),
            "attention_tensor": (
                "qr_done", "mla_w_used", "v_mla_done", "qr_turned",
            ),
            "attention_vector": (
                "qr_ready", "v_mla_ready", "qrT_ready",
            ),
            "pair_tensor": (
                "gate_done", "up_done", "down_done",
            ),
            "layer_tensor": (
                "rows_l_turned", "q2_done", "k2_done", "v2_done", "conf_mean", "conf_var", "ffn_done",
            ),
            "layer_scalar": (
                "lam_exp", "v2_ready", "o2_rms", "ln_rms",
            ),
            "layer_vector": (
                "cols_l_ready", "lam_dots", "o2_normed",
            ),
        }
        once_a_turn = {name: sem(group) for group, names in EACH_TURN.items() for name in names}
        turn_place = {name: (len(names), i + 1) for names in EACH_TURN.values() for i, name in enumerate(names)}

        def in_turn(eng, name, turn):
            per_turn, place = turn_place[name]
            eng.wait_ge(once_a_turn[name], turn * per_turn + place)

        block = ctx.enter_context(nc.Block())

        def arrived(eng, n, it=0, per=0):
            eng.wait_ge(landed[n % RING], it * (16 * per // RING) + 16 * (n // RING + 1))

        def parts_ready(eng, m, l):
            eng.wait_ge(lo_ready, l * PER_LAYER + RAW + m + 1)

        def parts_free(eng, m, l):
            eng.wait_ge(parts_used, l * PER_LAYER + m + 1)

        def split_k(w, m):
            return w[m % 2][:, :].rearrange("p (k n) -> p k n", k=KD)

        def split_wide(w, m):
            return w[m % 2][:, :].rearrange("p (k n) -> p k n", k=2)

        def kview(n):
            return ring[n % RING][:, :].rearrange("p (k n) -> p k n", k=KD)

        def wide(n):
            return ring[n % RING][:, :].rearrange("p (k n) -> p k n", k=2)

        def kcols(w, c0, n):
            return w[:, c0:c0 + n].rearrange("(k p) n -> p k n", p=P)

        w_in, w_mod = A["w_in"][0], A["w_mod"][0]
        heads_w = w_in[:, 0:4096].rearrange("(k p) (s h n) -> p k s h n", p=P, s=4, n=HD)

        @block.sync
        def _(sp):
            def load(n, dst, src, it=0, per=0, slots=1):
                if slots and (n >= RING or per):
                    sp.wait_ge(chunk_used, it * per + (n - RING + slots))
                sp.dma_start(dst, src).then_inc(landed[n % RING], 16)

            def load_head(h):
                for s in range(4):
                    src = heads_w[:, :, s, bass.ds(h, 1), :] if not isinstance(h, int) else heads_w[:, :, s, h:h + 1, :]
                    sp.dma_start(head_w[:, :, s * HD:(s + 1) * HD].unsqueeze(2), src).then_inc(sem("head_w_in"), 16)

            def load_mla(i):
                c = bass.ds(i * (2 * QK), 2 * QK) if not isinstance(i, int) else slice(0, 2 * QK)
                sp.dma_start(mla_wq[:], A["w_uq"][0][:, c].rearrange("(k p) n -> p k n", p=P)).then_inc(sem("mla_w_in"), 16)
                c = bass.ds(i * 512, 512) if not isinstance(i, int) else slice(0, 512)
                sp.dma_start(mla_wkv[:], A["w_ukv"][0][:, c].rearrange("(k p) n -> p k n", p=P)).then_inc(sem("mla_w_in"), 16)

            for j in range(8):
                load(N_MOD1 + j, kview(N_MOD1 + j), kcols(w_mod, j * 256, 256))
            load_head(0)
            ahead = []
            for j in range(2):
                ahead.append((N_LATENT + j, kcols(w_in, C_CQ + j * 256, 256)))
            ahead.append((N_LATENT + 2, kcols(w_in, C_CKV, 256)))
            for j in range(16):
                ahead.append((N_MOD2 + j, kcols(w_mod, 2048 + j * 256, 256)))
            for n, src in ahead[:8]:
                load(n, kview(n), src)
            with sp.Fori(1, HEADS) as h:
                in_turn(sp, "z_done", h - 1)
                load_head(h)
            sp.wait_ge(sem("head_done"), 1 + HEADS)
            load_mla(0)
            with sp.Fori(1, HEADS // 2) as i:
                in_turn(sp, "mla_w_used", i - 1)
                load_mla(i)
            for n, src in ahead[8:]:
                load(n, kview(n), src)
            sp.wait_ge(sem("mla_free"), 1 + HEADS // 2)
            sp.dma_start(gt1_b[:], A["b_mod"][0:1, 2048:3072].to_broadcast([P, DM])).then_inc(sem("gt1_in"), 16)
            with sp.Fori(0, 2) as half:
                for c in range(2):
                    col = half * 512 + c * 256
                    n = N_MERGE + 4 * c
                    parts = ((w_in, C_GATES), (A["w_o_dn"][0], 0), (w_in, C_GATES + DM), (A["w_o_mla"][0], 0))
                    for j, (w, c0) in enumerate(parts):
                        load(n + j, kview(n + j), w[:, bass.ds(col + c0, 256)].rearrange("(k p) n -> p k n", p=P), half, 8,
                             slots=0 if j % 2 else 2)
            for c in range(4):
                load(N_OUT + c, kview(N_OUT + c), kcols(A["w_out"][0], c * 256, 256))
            with sp.Fori(0, PAIRS) as pair:
                n = N_EXPERT
                for w in (A["w_gate"][0], A["w_up"][0], A["w_down"][0]):
                    for j in range(4):
                        for a in range(2):
                            src = w[bass.ds(pair * 2 + a, 1), j * 256:(j + 1) * 256, :].rearrange("e (k p) n -> p (e k) n", p=P)
                            load(n, wide(n), src, pair, PER_PAIR)
                            n += 1
            def load_raw(m, src, l, chunks=1):
                if chunks:
                    sp.wait_ge(lo_ready, l * PER_LAYER + m + chunks)
                dst = raw[m % RAW][:, :].rearrange("p (k n) -> p k n", k=2 if m >= M_DOWN else KD)
                sp.dma_start(dst, src).then_inc(raw_landed[m % RAW], 16)

            with sp.Fori(0, LAYERS) as l:
                m = M_IN
                wi = A["w_in_2"][bass.ds(l, 1)].rearrange("l k n -> (l k) n")
                for c0 in (2304, 2560, 256, 512, 0, 768, 1024, 1280, 1536, 1792, 2048):
                    load_raw(m, kcols(wi, c0, 256), l, {512: 2, 0: 0}.get(c0, 1))
                    m += 1
                wo = A["w_out_2"][bass.ds(l, 1)].rearrange("l k n -> (l k) n")
                for c in range(4):
                    load_raw(m, kcols(wo, c * 256, 256), l)
                    m += 1
                wg = A["w_gate_2"][bass.ds(l, 1)].rearrange("l k n -> (l k) n")
                wu = A["w_up_2"][bass.ds(l, 1)].rearrange("l k n -> (l k) n")
                for j in range(FB // 2):
                    for w in (wg, wu):
                        load_raw(m, kcols(w, j * 256, 256), l)
                        m += 1
                wd = A["w_down_2"][bass.ds(l, 1)].rearrange("l k n -> (l k) n")
                for j in range(FB // 2):
                    load_raw(m, wd[j * 256:(j + 1) * 256, :].rearrange("(k p) n -> p k n", p=P), l)
                    m += 1
            for t in range(TT):
                sp.wait_ge(sem("y_ready"), t + 1)
                sp.dma_start(out[0, t * P:(t + 1) * P, :], x[:, t, :]).then_inc(sem("stored"), 16)
            sp.wait_ge(sem("stored"), 16 * TT)

        @block.gpsimd
        def _(pool):
            pool.memset(ident[:], 0.0)
            pool.memset(tri[:], 1.0)
            pool.memset(chunk_ones[:], 0.0)
            pool.memset(level_blk[:], 1.0)
            pool.drain()
            pool.memset(chunk_ones[0:64, 0:64], 1.0)
            pool.drain()
            pool.memset(chunk_ones[64:128, 64:128], 1.0)
            pool.drain()
            pool.affine_select(out=ident[:], in_=ident[:], pattern=[[-1, P]], compare_op=ALU.not_equal, fill=1.0,
                               base=0, channel_multiplier=1).then_inc(step["ident_ready"], 1)
            pool.affine_select(out=tri[:, 0, :], in_=tri[:, 0, :], pattern=[[1, P]], compare_op=ALU.is_ge, fill=0.0,
                               base=0, channel_multiplier=-1)
            pool.affine_select(out=tri[:, 1, :], in_=tri[:, 1, :], pattern=[[-1, P]], compare_op=ALU.is_ge, fill=0.0,
                               base=0, channel_multiplier=1)
            for i in range(7):
                s = 1 << i
                blk = level_blk[:, i, :].rearrange("p (b s) -> p b s", s=s)
                pool.affine_select(out=blk, in_=blk, pattern=[[-s, P // s], [0, s]], compare_op=ALU.is_ge, fill=0.0,
                                   base=0, channel_multiplier=1)
            pool.drain()
            pool.memset(tri[0:64, 0, 64:128], 0.0)
            pool.drain()
            pool.memset(tri[64:128, 1, 0:64], 0.0)
            pool.drain()
            for i in range(7):
                s = 1 << i
                blk = level_blk[:, i, :].rearrange("p (b s) -> p b s", s=s)
                pool.affine_select(out=blk, in_=blk, pattern=[[s, P // s], [0, s]], compare_op=ALU.is_ge, fill=0.0,
                                   base=s - 1, channel_multiplier=-1)
            pool.drain()
            for i in range(6):
                last = pool.tensor_tensor(level_mask[:, i, :], level_blk[:, i + 1, :], level_blk[:, i, :], ALU.subtract)
            last.then_inc(step["masks_ready"], 1)

            with pool.Fori(0, HEADS) as h:
                pool.wait_ge(sem("head_done"), h + 1)
                in_turn(pool, "k_tok_ready", h)
                in_turn(pool, "head_q_ready", h)
                in_turn(pool, "v_tok_ready", h)

                def scaled(dst, src, qty, d):
                    col = head_q[:, qty, :].rearrange("p (t d) -> p t d", d=2)[:, :, d:d + 1].to_broadcast([P, TT, P])
                    return pool.tensor_tensor(dst[:, d], src[:], col, ALU.mult)

                for d in range(2):
                    scaled(v_beta, v_tok, 0, d)
                    scaled(k_beta, k_tok, 2, d)
                    scaled(k_state, k_tok, 3, d).then_inc(sem("scaled_ready"), 1)
                for lv in range(6):
                    for d in range(2):
                        if lv == 0:
                            pool.wait_ge(sem("L_ready"), h * 2 + d + 1)
                        elif lv == 1:
                            pool.wait_ge(sem("T_ready"), h * 12 + d + 1)
                        else:
                            pool.wait_ge(sem("n_done"), h * 12 + 2 * (lv - 1) + d + 1)
                        mask = level_mask[:, lv:lv + 1, :].to_broadcast([P, TT, P])
                        pool.tensor_tensor(solve_C[:, d], e_L[:, d], mask, ALU.mult).then_inc(sem("C_ready"), 1)

            pool.wait_ge(sem("x_ready"), 1)
            pool.memset(onehot[:, :, PAIRS * P:], 0.0)
            pool.iota(iota64[:], pattern=[[1, 64]], base=0, channel_multiplier=0, allow_small_or_imprecise_dtypes=True)
            for a in range(2):
                pool.drain()
                pool.iota(iota_p[a * 64:a * 64 + 64, :], pattern=[[0, 1]], base=0, channel_multiplier=1,
                          allow_small_or_imprecise_dtypes=True)
            pool.drain()
            pool.memset(pair_sel[:], 0.0)
            pool.memset(zeros16[:], 0.0)
            pool.drain()
            sel = pair_sel[:].rearrange("k r (a n) -> k r a n", a=2)
            pool.affine_select(out=sel, in_=sel, pattern=[[-2, PAIRS], [-1, 2], [0, 64]], compare_op=ALU.not_equal,
                               fill=1.0, base=0, channel_multiplier=1)
            pool.drain().then_inc(step["route_consts"], 1)

            pool.wait_ge(chunk_used, N_LAYER - RING + RAW)
            pool.sem_inc(lo_ready, RAW)

            pool.wait_ge(sem("x_ready"), 2)
            pool.memset(causal[:], 0.0)
            pool.memset(ones[:], 1.0)
            pool.drain()
            pool.affine_select(out=causal[:], in_=causal[:], pattern=[[-1, P]], compare_op=ALU.is_ge, fill=-1e30,
                               base=0, channel_multiplier=1)
            pool.drain().then_inc(step["block2_consts"], 1)
            with pool.Fori(0, LAYERS * PER_LAYER // RAW) as g:
                for i in range(RAW):
                    pool.wait_ge(hi_ready, g * RAW + i + 1)
                    pool.tensor_tensor(w_lo[i % 2][:], raw[i][:], w_hi[i % 2][:].bitcast(F32), ALU.subtract).then_inc(lo_ready, 1)

        @block.scalar
        def _(act):
            def copy(dst, src):
                return act.activation(dst, src, ACT.Copy)

            def flat(ap):
                return ap.rearrange("(r p) -> r p", p=P)

            rows = ((R_C, A["c"][0]), (R_BMOD, A["b_mod"][0]), (R_GMIX, A["g_mix"][0]), (R_GFFN, A["g_ffn"][0]),
                    (R_QG, A["q_gain"][0]), (R_KVG, A["kv_gain"][0]), (R_OG, A["dn_o_gain"][0]))
            for r0, v in rows:
                n = v.shape[0] // P
                act.dma_start(rows_a[r0:r0 + n, :], flat(v)).then_inc(sem("rows_in"), 16)
            act.dma_start(rows_b[:], A["conv_w"][0].rearrange("j (b p) -> (j b) p", p=P)).then_inc(sem("rows_in"), 16)
            for t in range(TT):
                act.dma_start(x[:, t, :], A["x"][0, t * P:(t + 1) * P, :]).then_inc(sem("x_in"), 16)
            act.dma_start(w_small[:, :, 0:32], kcols(w_in, C_B, 32)).then_inc(sem("w_small_in"), 16)
            act.dma_start(w_small[:, :, 32:96], kcols(w_in, C_KR, 64)).then_inc(sem("w_small_in"), 16)
            for i, name in enumerate(("positions", "positions_2")):
                act.dma_start(pos_i[:, 4 * i:4 * i + 4], A[name].rearrange("a (t p) -> p (a t)", p=P), allow_slow_non_contiguous=True).then_inc(sem("aux_in"), 16)
            act.dma_start(inv_freq[:], A["inv_freq"].to_broadcast([P, 32])).then_inc(sem("aux_in"), 16)
            act.dma_start(a_log_b[:], A["a_log"].rearrange("l a h -> l (a h)").to_broadcast([P, 16])).then_inc(sem("aux_in"), 16)
            act.dma_start(dt_b[:], A["dt_bias"].rearrange("l a h -> l (a h)").to_broadcast([P, 16])).then_inc(sem("aux_in"), 16)
            act.dma_start(w_router[:], A["w_router"][0].rearrange("(k p) e -> p k e", p=P)).then_inc(sem("w_router_in"), 16)
            act.dma_start(gt2_b[:], A["b_mod"][0:1, 5120:6144].to_broadcast([P, DM])).then_inc(sem("gt2_in"), 16)

            reached(act, "cols_ready")
            act.activation(silu_c[:], cols_a[:, R_C:R_C + KD], ACT.Silu).then_inc(step["silu_c_ready"], 1)
            reached(act, "angles_ready")
            act.activation(sin[:], sin[:], ACT.Sin)
            act.activation(cos[:], cos[:], ACT.Sin).then_inc(step["rope_ready"], 1)

            def norm_sums(n):
                for t in range(TT):
                    if isinstance(n, int) and n == 0:
                        act.wait_ge(sem("x_in"), 16 * TT)
                    elif t == 0:
                        act.wait_ge(sem("x_ready"), n)
                    act.activation(xn[:, t, :], x[:, t, :], ACT.Square, accum_out=ss[:, t:t + 1])
                act.drain()
                act.activation(rms[:, 0:TT], ss[:, 0:TT], ACT.Sqrt, scale=1.0 / DM, bias=eps_col[:, 0:1]).then_inc(sem("rms_ready"), 1)

            def norm_turned(n, gain, shift):
                for k in range(1, KD, 2):
                    act.wait_ge(sem("turned"), n * KD + k + 1)
                    act.activation(hT[:, k, :], bank[4 + k % 4][:], ACT.Identity, scale=gain(k),
                                   bias=0.0 if shift is None else shift(k)).then_inc(sem("hT_act"), 1)

            reached(act, "eps_ready")
            norm_sums(0)
            reached(act, "mod1_cols")
            norm_turned(0, lambda k: mod_g1[:, k:k + 1], lambda k: mod_sh1[:, k:k + 1])

            reached(act, "small_done")
            for t in range(TT):
                last = copy(small[:, t, :], bank[0][:, t * 96:(t + 1) * 96])
            last.then_inc(step["small_ready"], 1)
            act.drain()
            beta = col_q[:, 0].rearrange("p (t d) h -> p t (d h)", t=TT)
            act.activation(beta, small[:, :, 0:16], ACT.Sigmoid)
            reached(act, "sp_in")
            act.activation(sp_b[:], sp_b[:], ACT.Exp, scale=-1.0)
            act.activation(a_log_b[:], a_log_b[:], ACT.Exp)
            act.drain()
            act.activation(sp_b[:], sp_b[:], ACT.Ln, bias=1.0).then_inc(step["sp_ready"], 1)
            reached(act, "gc_ready")
            act.activation(col_q[:, 2], col_q[:, 1], ACT.Exp)
            act.activation(col_q[:, 3], col_q[:, 3], ACT.Exp).then_inc(step["gc_exp"], 1)

            act.sem_inc(sem("head_done"), 1)
            with act.Fori(0, HEADS) as h:
                for s in range(3):
                    act.wait_ge(sem("conv_done"), h * 3 + s + 1)
                    act.activation(conv_out[:, s, :], conv_out[:, s, :], ACT.Silu).then_inc(sem("silu_done"), 1)
                in_turn(act, "z_done", h)
                act.activation(z_silu[:].rearrange("p t n -> p (t n)"), bank[3][:], ACT.Silu).then_inc(once_a_turn["z_ready"], 1)
                for s in range(2):
                    act.wait_ge(sem("tok_done"), h * 3 + s + 1)
                    for t in range(TT):
                        act.activation(v_beta[:, s, t, :], bank[4 + s][:, t * P:(t + 1) * P], ACT.Square,
                                       accum_out=ss[:, s * 4 + t:s * 4 + t + 1])
                act.drain()
                act.activation(rms[:, 0:8], ss[:, 0:8], ACT.Sqrt, bias=eps_col[:, 0:1]).then_inc(once_a_turn["len_ready"], 1)
                act.wait_ge(sem("tok_done"), h * 3 + 3)
                copy(v_tok[:].rearrange("p t n -> p (t n)"), bank[6][:]).then_inc(once_a_turn["v_tok_ready"], 1)
                for d in range(2):
                    act.wait_ge(sem("gc_row_done"), h * 2 + d + 1)
                    act.activation(e_row[:, d, :], bank[7 if d == 0 else 2][:], ACT.Exp).then_inc(sem("e_row_ready"), 1)
                    act.wait_ge(sem("e_arg_ready"), h * 2 + d + 1)
                    act.activation(e_T[:, d], e_T[:, d], ACT.Exp)
                    act.activation(e_L[:, d], e_L[:, d], ACT.Exp, scale=-1.0).then_inc(sem("e_ready"), 1)
                for s, dst in enumerate((qnT, knT)):
                    act.wait_ge(sem("nT_done"), h * 2 + s + 1)
                    copy(dst[:], bank[s][:]).then_inc(sem("nT_ready"), 1)
                for lv in range(1, 6):
                    for d in range(2):
                        act.wait_ge(sem("n_done"), h * 12 + 2 * lv + d + 1)
                        copy(solve_N[:, d, :], bank[d][:]).then_inc(sem("n_ready"), 1)
                for d in range(2):
                    act.wait_ge(sem("u_done"), h * 2 + d + 1)
                    copy(u[:, d].rearrange("p t n -> p (t n)"), bank[3 if d == 0 else 6][:]).then_inc(sem("u_ready"), 1)
                    act.wait_ge(sem("w_done"), h * 2 + d + 1)
                    copy(wT[:, d, :], bank[4 + d][:]).then_inc(sem("w_ready"), 1)
                act.wait_ge(sem("o_done"), h * 2 + 1)
                copy(o_tok[:].rearrange("p t n -> p (t n)"), bank[7][:]).then_inc(once_a_turn["o_fwd_ready"], 1)
                in_turn(act, "o_sum", h)
                for t in range(TT):
                    act.activation(v_beta[:, 0, t, :], o_tok[:, t, :], ACT.Square, accum_out=ss[:, t:t + 1])
                act.drain()
                act.activation(rms[:, 0:TT], ss[:, 0:TT], ACT.Sqrt, scale=1.0 / HD, bias=eps_col[:, 0:1]).then_inc(once_a_turn["o_rms"], 1)
                in_turn(act, "oT_done", h)
                act.activation(oT_dn[:, bass.ds(h, 1), :].rearrange("p a n -> p (a n)"), bank[0][:], ACT.Copy,
                               scale=cols_a[:, R_OG:R_OG + 1]).then_inc(sem("head_done"), 1)

            reached(act, "latent_done")
            for t in range(TT):
                act.activation(xn[:, t, 0:512], bank[t][:], ACT.Square, accum_out=ss[:, t:t + 1])
                act.activation(xn[:, t, 512:768], bank[4 + t // 2][:, (t % 2) * 256:(t % 2) * 256 + 256], ACT.Square,
                               accum_out=ss[:, 4 + t:5 + t])
            act.drain()
            act.activation(rms[:, 0:4], ss[:, 0:4], ACT.Sqrt, scale=1.0 / Q_LORA, bias=eps_col[:, 0:1])
            act.activation(rms[:, 4:8], ss[:, 4:8], ACT.Sqrt, scale=1.0 / KV_LORA, bias=eps_col[:, 0:1]).then_inc(step["latent_rms"], 1)
            for b in range(6):
                act.wait_ge(sem("latent_turned"), b + 1)
                g = cols_a[:, R_QG + b:R_QG + b + 1]
                dst = cqT[:, b, :] if b < 4 else ckvT[:, b - 4, :]
                act.activation(dst, bank[b][:], ACT.Copy, scale=g).then_inc(sem("latent_T"), 1)
            reached(act, "kr_done")
            copy(krT[:], bank[6][:]).then_inc(step["krT_ready"], 1)
            act.sem_inc(sem("mla_free"), 1)
            scale = float(QK) ** -0.5
            with act.Fori(0, HEADS // 2) as i:
                for a in range(2):
                    act.wait_ge(sem("qk_done"), i * 4 + a + 1)
                    copy(qT[:, a, :], bank[a][:]).then_inc(sem("qk_ready"), 1)
                for a in range(2):
                    act.wait_ge(sem("qk_done"), i * 4 + a + 3)
                    copy(kT[:, a, :], bank[3 + a][:]).then_inc(sem("qk_ready"), 1)

                def evac_probs(n):
                    act.wait_ge(sem("p_turned"), i * 8 + n + 1)
                    dst = pT[:, n // 4, :, (n % 4) * P:(n % 4 + 1) * P]
                    copy(dst, bank[4 + n % 2][:].rearrange("p (k q) -> p k q", k=TT)).then_inc(sem("pT_ready"), 1)

                for n in range(8):
                    act.wait_ge(sem("nmax_ready"), i * 8 + n + 1)
                    if n >= 2:
                        act.wait_ge(sem("p_turned"), i * 8 + n - 1)
                    act.activation(probs[:, n % 2, :], bank[n % 4][:], ACT.Exp, scale=scale, bias=nmax[:, n % 2:n % 2 + 1],
                                   accum_out=psums[:, n % 2:n % 2 + 1]).then_inc(sem("exp_done"), 1)
                    if n >= 1:
                        evac_probs(n - 1)
                evac_probs(7)
                for a in range(2):
                    act.wait_ge(sem("pv_done"), i * 2 + a + 1)
                    last = copy(oT_mla[:, bass.ds(i * 2 + a, 1), :].rearrange("p a n -> p (a n)"), bank[6 + a][:])
                last.then_inc(sem("mla_free"), 1)

            with act.Fori(0, 2) as half:
                for c in range(2):
                    for j in range(2):
                        for b in range(2):
                            act.wait_ge(sem("merge_done"), half * 8 + c * 4 + j * 2 + b + 1)
                            act.wait_ge(sem("sig_free"), half * 4 + c * 2 + b + 1)
                            act.activation(sig[:, b, j, :], bank[b * 4 + 2 * j][:], ACT.Sigmoid).then_inc(sem("sig_ready"), 1)

            norm_sums(1)
            reached(act, "mod2_cols")
            norm_turned(1, lambda k: mod_g2[:, k:k + 1], lambda k: mod_sh2[:, k:k + 1])
            reached(act, "amax_ready")
            for t in range(TT):
                act.activation(aff[:, t, :], bank[0][:, t * 16:(t + 1) * 16], ACT.Exp, bias=amax[:, t:t + 1],
                               accum_out=asum[:, t:t + 1])
            act.drain().then_inc(step["aff_exp"], 1)
            for g in range(PAIRS):
                act.wait_ge(sem("scat_rows"), g + 1)
                if g >= 2:
                    act.wait_ge(sem("scat_ready"), g - 1)
                copy(gate_b[:, g % 2, :], bank[2 * (g % 2) + 1][:]).then_inc(sem("gate_b_ready"), 1)

            act.dma_start(gfin_b[:], A["g_final"].rearrange("(a n) -> a n", a=1).to_broadcast([P, DM])).then_inc(sem("gfin_in"), 16)
            act.dma_start(gfin2_b[:], A["final_norm_g_2"].rearrange("(a n) -> a n", a=1).to_broadcast([P, DM])).then_inc(sem("gfin_in"), 16)

            def gathered(n):
                act.wait_ge(sem("gather_done"), n)
                for k in range(4, 8):
                    last = act.activation(xeT[:, k, :], bank[5][:, (k - 4) * P:(k - 3) * P], ACT.Identity,
                                          scale=mod_g2[:, k:k + 1], bias=mod_sh2[:, k:k + 1])
                last.then_inc(sem("xeT_act"), 1)

            gathered(1)
            with act.Fori(0, PAIRS) as pair:
                in_turn(act, "gate_done", pair)
                for hf in range(2):
                    act.activation(hid[:, hf * 512:(hf + 1) * 512], bank[hf][:], ACT.Silu).then_inc(sem("silu_hid"), 1)
                gathered(pair + 2)
                act.wait_ge(sem("hid_turned"), pair * 2 + 1)
                copy(hidT[:, 0:4, :].rearrange("p k n -> p (k n)"), bank[0][:]).then_inc(sem("hidT_act"), 1)
                in_turn(act, "down_done", pair)
                copy(ye[:, bass.ds(pair, 1), 0:512].rearrange("p a n -> p (a n)"), bank[6][:]).then_inc(sem("ye_act"), 1)

            def final_rms(name, gate):
                gate()
                for t in range(TT):
                    act.activation(xn[:, t, :], x[:, t, :], ACT.Square, accum_out=ss[:, t:t + 1])
                act.drain()
                act.activation(rms[:, 0:TT], ss[:, 0:TT], ACT.Sqrt, scale=1.0 / DM, bias=eps_col[:, 0:1]).then_inc(step[name], 1)

            final_rms("first_rms", lambda: reached(act, "x_first"))

            act.sem_inc(sem("rows_l_free"), 1)

            def split(m):
                act.wait_ge(raw_landed[m % RAW], l * (16 * PER_LAYER // RAW) + 16 * (m // RAW + 1))
                parts_free(act, m, l)
                copy(w_hi[m % 2][:], raw[m % RAW][:]).then_inc(hi_ready, 1)

            def turned_hi(n, gain):
                for k in range(KD):
                    act.wait_ge(sem("turned"), (n + 2) * KD + k + 1)
                    act.activation(hT_hi[:, k, :], bank[4 + k % 4][:], ACT.Copy, scale=gain(k)).then_inc(sem("hT_hi_ready"), 1)

            def split_hid(j):
                act.wait_ge(sem("ffn_hid"), l * FB + 2 * j + 2)
                parts_free(act, M_DOWN + j, l)
                copy(ffn_hi[:, j % 2], ffn_hT[:, 2 * j:2 * j + 2, :]).then_inc(sem("ffn_hi_ready"), 1)

            with act.Fori(0, LAYERS) as l:
                split(0)
                split(1)
                act.wait_ge(sem("x_ready"), l * 2 + 2)
                act.wait_ge(sem("rows_l_free"), l + 1)
                rows = ((L_MIX, "mix_norm_g_2"), (L_FFN, "ffn_norm_g_2"), (L_GLU, "glu_b_2"), (L_DWB, "conf_dw_b_2"),
                        (L_LNG, "conf_ln_g_2"), (L_LNB, "conf_ln_b_2"), (L_SUB, "diff_subln_g_2"))
                for r0, name in rows:
                    n = A[name].shape[1] // P
                    act.dma_start(rows_l[r0:r0 + n, :], A[name][bass.ds(l, 1)].rearrange("l (r p) -> (l r) p", p=P))\
                        .then_inc(sem("rows_l_in"), 16)
                for r0, name in ((L_SC, "short_conv_w_2"), (L_DW, "conf_dw_w_2")):
                    n = A[name].shape[1] * 2
                    act.dma_start(rows_l[r0:r0 + n, :], A[name][bass.ds(l, 1)].rearrange("l j (b p) -> (l j b) p", p=P))\
                        .then_inc(sem("rows_l_in"), 16)
                for j, name in enumerate(("lam_q1_2", "lam_k1_2", "lam_q2_2", "lam_k2_2")):
                    act.dma_start(lam_in[:, j, :], A[name][bass.ds(l, 1)].to_broadcast([P, 64])).then_inc(sem("rows_l_in"), 16)
                norm_sums(l * 2 + 2)
                in_turn(act, "cols_l_ready", l)
                turned_hi(l * 2, lambda k: cols_l[:, L_MIX + k:L_MIX + k + 1])
                in_turn(act, "lam_dots", l)
                act.activation(lam_s[:, 0:2], lam_s[:, 0:2], ACT.Exp).then_inc(once_a_turn["lam_exp"], 1)
                split(2)
                split(3)
                for b in range(2):
                    act.wait_ge(sem("proj_done"), l * 10 + 3 + b)
                    act.activation(sig2[:, b, :], bank[2 + b][:], ACT.Sigmoid, bias=cols_l[:, L_GLU + 2 + b:L_GLU + 3 + b])\
                        .then_inc(sem("glu_sig"), 1)
                split(4)
                for b in range(2):
                    act.wait_ge(sem("proj_done"), l * 10 + 5 + b)
                    copy(prod[:, b, 2:], bank[4 + b][:]).then_inc(sem("ac_ready"), 1)
                for m in range(5, M_OUT):
                    split(m)
                for j in range(2):
                    dst = q2T if j == 0 else k2T
                    if j == 1:
                        split(M_OUT)
                        split(M_OUT + 1)
                    for b in range(4):
                        act.wait_ge(sem("qk2_turned"), l * 8 + j * 4 + b + 1)
                        copy(dst[:, b, :], bank[(4 if j == 0 else 0) + b][:]).then_inc(sem("qk2T_ready"), 1)
                in_turn(act, "v2_done", l)
                for t in range(TT):
                    last = copy(v2[:, t, :], bank[4 + t][:])
                last.then_inc(once_a_turn["v2_ready"], 1)

                def exps(n):
                    w = (n % 4 + 1) * P
                    for m in range(2):
                        j = (n % 2) * 2 + m
                        act.wait_ge(sem("nmax2_ready"), l * 32 + 2 * n + m + 1)
                        act.activation(p2[:, j, 0:w], bank[j][:, 0:w], ACT.Exp, scale=0.125, bias=nmax2[:, j:j + 1],
                                       accum_out=psum2[:, j:j + 1]).then_inc(sem("exp2_done"), 1)

                def evac_a(n):
                    w = n % 4 + 1
                    act.wait_ge(sem("a_turned"), l * 16 + n + 1)
                    copy(aT[:, n % 2, 0:w, :], bank[4 + n % 2][:, 0:w * P].rearrange("p (k q) -> p k q", k=w))\
                        .then_inc(sem("aT_ready"), 1)

                def evac_o(n):
                    act.wait_ge(sem("pv2_done"), l * 16 + n + 1)
                    act.activation(o2[:, n % 4, n // 4, :], bank[6 + n % 2][:, 0:P], ACT.Copy).then_inc(sem("o2_ready"), 1)

                for n in range(16):
                    exps(n)
                    if n >= 1:
                        evac_a(n - 1)
                    if n >= 2:
                        evac_o(n - 2)
                evac_a(15)
                evac_o(14)
                evac_o(15)
                act.drain()
                for n in range(16):
                    act.activation(p2[:, n // 4, n % 4 * P:(n % 4 + 1) * P], o2[:, n % 4, n // 4, :], ACT.Square, accum_out=ss[:, n:n + 1])
                act.drain()
                act.activation(rms[:], ss[:], ACT.Sqrt, scale=1.0 / VD, bias=eps_col[:, 0:1]).then_inc(once_a_turn["o2_rms"], 1)
                for b in range(2):
                    act.wait_ge(sem("conf_centred"), l * 2 + b + 1)
                    act.activation(conv_acc[:, b, :], conf[:, b, :], ACT.Square).then_inc(sem("conf_sq"), 1)
                in_turn(act, "conf_var", l)
                act.activation(ln_rs[:], bank[1][:], ACT.Sqrt, scale=1.0 / 256, bias=eps_col[:, 1:2]).then_inc(once_a_turn["ln_rms"], 1)
                for b in range(4):
                    act.wait_ge(sem("o2_turned"), l * 4 + b + 1)
                    act.activation(yT_hi[:, 2 + b, :], bank[4 + b][:], ACT.Copy, scale=lam_i[:, 1:2]).then_inc(sem("yT_hi_ready"), 1)
                for b in range(2):
                    act.wait_ge(sem("conf_normed"), l * 2 + b + 1)
                    act.activation(conv_acc[:, b, :], conf[:, b, :], ACT.Silu, scale=cols_l[:, L_LNG + b:L_LNG + b + 1],
                                   bias=cols_l[:, L_LNB + b:L_LNB + b + 1])
                act.drain()
                for b in range(2):
                    copy(yT_hi[:, 6 + b, :], conv_acc[:, b, :]).then_inc(sem("yT_hi_ready"), 1)
                for m in range(M_OUT + 2, M_UP + 2):
                    split(m)
                norm_sums(l * 2 + 3)
                turned_hi(l * 2 + 1, lambda k: cols_l[:, L_FFN + k:L_FFN + k + 1])
                for j in range(FB // 2):
                    split(M_UP + 2 * j + 2)
                    for f in range(2 * j, 2 * j + 2):
                        act.wait_ge(sem("ffn_gate"), l * FB + f + 1)
                        if f >= 4:
                            act.wait_ge(sem("ffn_hid"), l * FB + f - 3)
                        act.activation(ffn_sg[:, f % 4, :], bank[(f // 2 % 2) * 4 + f % 2][:], ACT.Silu).then_inc(sem("ffn_silu"), 1)
                    split(M_UP + 2 * j + 3)
                    if j >= FB // 2 - 2:
                        split_hid(j - (FB // 2 - 2))
                for j in range(2, FB // 2):
                    split(M_DOWN + j)
                    split_hid(j)
            final_rms("last_rms", lambda: act.wait_ge(sem("x_ready"), 2 + 2 * LAYERS))

        @block.tensor
        def _(pe):
            mm = pe.matmul

            def blocks(dst, n, b, it=0, per=0):
                for k in range(KD):
                    last = mm(dst, kview(n)[:, k, b * P:(b + 1) * P], hT[:, k, :], start=k == 0, stop=k == KD - 1)
                return last

            def norm_turn(n, parts=None):
                for k in range(KD):
                    if k == 0:
                        pe.wait_ge(sem("xn_ready"), n + 1)
                    if k >= 4 and parts is not None:
                        pe.wait_ge(sem("hT_lo_ready"), parts * KD + k - 3)
                    elif k >= 4:
                        pe.wait_ge(sem("hT_act" if k % 2 else "hT_dve"), n * 4 + (k - 4) // 2 + 1)
                    for t in range(TT):
                        last = pe.transpose(bank[4 + k % 4][:, t * P:(t + 1) * P], xn[:, t, k * P:(k + 1) * P], ident[:])
                    last.then_inc(sem("turned"), 1)

            def normed(n):
                pe.wait_ge(sem("hT_act"), n * 4 + 4)
                pe.wait_ge(sem("hT_dve"), n * 4 + 4)

            reached(pe, "ident_ready")
            pe.wait_ge(sem("rows_in"), 16 * 8)
            pe.transpose(bank[6][:, 0:R_A], rows_a[:], ident[0:R_A, 0:R_A])
            pe.transpose(bank[7][:, 0:CONV_K * 24], rows_b[:], ident[0:CONV_K * 24, 0:CONV_K * 24]).then_inc(step["rows_turned"], 1)

            def mod_cols(n, dst):
                arrived(pe, n)
                for b in range(2):
                    for k in range(KD):
                        last = mm(dst[:, b:b + 1], kview(n)[:, k, b * P:(b + 1) * P], silu_c[:, k:k + 1],
                                  start=k == 0, stop=k == KD - 1)
                return last.then_inc(chunk_used, 1)

            reached(pe, "silu_c_ready")
            for j in range(8):
                mod_cols(N_MOD1 + j, bank[0][:, 2 * j:2 * j + 2])
            pe.drain().then_inc(step["mod1_done"], 1)
            norm_turn(0)
            normed(0)

            pe.wait_ge(sem("w_small_in"), 32)
            reached(pe, "mod1_cols")
            for t in range(TT):
                for k in range(KD):
                    last = mm(bank[0][:, t * 96:(t + 1) * 96], hT[:, k, t * P:(t + 1) * P], w_small[:, k, :],
                              start=k == 0, stop=k == KD - 1)
            last.then_inc(step["small_done"], 1)
            reached(pe, "g_ready")
            for t in range(TT):
                for d in range(2):
                    g = col_q[:, 4, 2 * t + d, :]
                    mm(bank[1][:, t * 16 + d * 8:t * 16 + d * 8 + 8], tri[:, d, :], g, start=True, stop=True)
                    last = mm(bank[2][:, t * 16 + d * 8:t * 16 + d * 8 + 8], chunk_ones[:], g, start=True, stop=True)
            last.then_inc(step["gc_done"], 1)

            reached(pe, "gc_exp")
            with pe.Fori(0, HEADS) as h:
                pe.wait_ge(sem("head_done"), h + 1)
                pe.wait_ge(sem("head_w_in"), h * 64 + 64)
                for s in range(3):
                    for k in range(KD):
                        last = mm(bank[s][:], head_w[:, k, s * HD:(s + 1) * HD], hT[:, k, :], start=k == 0, stop=k == KD - 1)
                    last.then_inc(sem("qkv_done"), 1)
                for t in range(TT):
                    for k in range(KD):
                        last = mm(bank[3][:, t * P:(t + 1) * P], hT[:, k, t * P:(t + 1) * P], head_w[:, k, 3 * HD:4 * HD],
                                  start=k == 0, stop=k == KD - 1)
                last.then_inc(once_a_turn["z_done"], 1)
                for s in range(3):
                    pe.wait_ge(sem("silu_done"), h * 3 + s + 1)
                    for t in range(TT):
                        last = pe.transpose(bank[4 + s][:, t * P:(t + 1) * P], conv_out[:, s, t * P:(t + 1) * P], ident[:])
                    last.then_inc(sem("tok_done"), 1)
                in_turn(pe, "g_wide_ready", h)
                for d in range(2):
                    for t in range(TT):
                        last = mm(bank[7 if d == 0 else 2][:, t * P:(t + 1) * P], g_wide[:, t, d, :], tri[:, d, :], start=True, stop=True)
                    last.then_inc(sem("gc_row_done"), 1)
                for s, src in enumerate((q_tok, k_tok)):
                    in_turn(pe, "q_tok_ready" if s == 0 else "k_tok_ready", h)
                    for t in range(TT):
                        last = pe.transpose(bank[s][:, t * P:(t + 1) * P], src[:, t, :], ident[:])
                    last.then_inc(sem("nT_done"), 1)
                pe.wait_ge(sem("nT_ready"), h * 2 + 2)
                in_turn(pe, "z_ready", h)
                for t in range(TT):
                    c = slice(t * P, (t + 1) * P)
                    last = mm(bank[3][:, c], knT[:, c], knT[:, c], start=True, stop=True)
                last.then_inc(once_a_turn["kk_done"], 1)
                in_turn(pe, "v_tok_ready", h)
                for t in range(TT):
                    c = slice(t * P, (t + 1) * P)
                    last = mm(bank[6][:, c], knT[:, c], qnT[:, c], start=True, stop=True)
                last.then_inc(once_a_turn["kq_done"], 1)
                for d in range(2):
                    pe.wait_ge(sem("C_ready"), h * 12 + d + 1)
                    for t in range(TT):
                        last = pe.transpose(bank[d][:, t * P:(t + 1) * P], solve_C[:, d, t, :], ident[:])
                    last.then_inc(sem("n_done"), 1)
                pe.wait_ge(sem("e_row_ready"), h * 2 + 2)
                for lv in range(1, 6):
                    for d in range(2):
                        pe.wait_ge(sem("C_ready"), h * 12 + 2 * lv + d + 1)
                        pe.wait_ge(sem("T_ready"), h * 12 + 2 * (lv - 1) + d + 1)
                        for t in range(TT):
                            c = slice(t * P, (t + 1) * P)
                            last = mm(bank[d][:, c], solve_C[:, d, t, :], solve_TT[:, d, c], start=True, stop=True)
                        last.then_inc(sem("n_done"), 1)
                    for d in range(2):
                        pe.wait_ge(sem("n_ready"), h * 10 + 2 * (lv - 1) + d + 1)
                        for t in range(TT):
                            c = slice(t * P, (t + 1) * P)
                            last = mm(bank[7 if d == 0 else 2][:, c], solve_T[:, d, c], solve_N[:, d, c], start=True, stop=True)
                        last.then_inc(sem("dTT_done"), 1)
                        if lv < 5:
                            for t in range(TT):
                                c = slice(t * P, (t + 1) * P)
                                last = mm(bank[4 + d][:, c], solve_N[:, d, c], solve_T[:, d, c], start=True, stop=True)
                            last.then_inc(sem("dT_done"), 1)
                pe.wait_ge(sem("scaled_ready"), h * 2 + 2)
                for d in range(2):
                    pe.wait_ge(sem("T_ready"), h * 12 + 10 + d + 1)
                    for t in range(TT):
                        c = slice(t * P, (t + 1) * P)
                        last = mm(bank[3 if d == 0 else 6][:, c], solve_TT[:, d, c], v_beta[:, d, t, :], start=True, stop=True)
                    last.then_inc(sem("u_done"), 1)
                    for t in range(TT):
                        c = slice(t * P, (t + 1) * P)
                        last = mm(bank[4 + d][:, c], k_beta[:, d, t, :], solve_TT[:, d, c], start=True, stop=True)
                    last.then_inc(sem("w_done"), 1)
                pe.wait_ge(sem("w_ready"), h * 2 + 2)
                pe.wait_ge(sem("q_dec_ready"), h * 2 + 2)
                for s in range(8):
                    for d in range(2):
                        c = s if d == 0 else 7 - s
                        t, r0 = c // 2, c % 2 * 64
                        rs, tc = slice(r0, r0 + 64), slice(c * 64, c * 64 + 64)
                        pe.wait_ge(sem("state_ready"), h * 16 + 2 * s + d + 1)
                        mm(bank[d][rs, 0:P], wT[:, d, tc], state[:, d, :], start=True, stop=True).then_inc(sem("ws_done"), 1)
                        if s < 7:
                            mm(bank[7 if d == 0 else 2][rs, t * P:(t + 1) * P], q_decT[:, d, tc], state[:, d, :], start=True, stop=False)
                    for d in range(2):
                        c = s if d == 0 else 7 - s
                        t, r0 = c // 2, c % 2 * 64
                        rs, tc = slice(r0, r0 + 64), slice(c * 64, c * 64 + 64)
                        o_out = bank[7 if d == 0 else 2][rs, t * P:(t + 1) * P]
                        pe.wait_ge(sem("v_new_ready"), h * 16 + 2 * s + d + 1)
                        if s < 7:
                            mm(bank[4 + d][:, 0:P], k_state[rs, d, t, :], v_new[rs, d, :], start=True, stop=True).then_inc(sem("ds_done"), 1)
                        else:
                            mm(o_out, q_decT[:, d, tc], state[:, d, :], start=True, stop=False)
                        last = mm(o_out, e_T[rs, d, t, r0:r0 + 64], v_new[rs, d, :], start=False, stop=True)
                        if s == 7:
                            last.then_inc(sem("o_done"), 1)
                in_turn(pe, "o_ready", h)
                for t in range(TT):
                    last = pe.transpose(bank[0][:, t * P:(t + 1) * P], o_tok[:, t, :], ident[:])
                last.then_inc(once_a_turn["oT_done"], 1)

            pe.wait_ge(sem("head_done"), 1 + HEADS)
            for j in range(2):
                arrived(pe, N_LATENT + j)
                for t in range(TT):
                    for k in range(KD):
                        last = mm(bank[t][:, j * 256:(j + 1) * 256], hT[:, k, t * P:(t + 1) * P], kview(N_LATENT + j)[:, k, :],
                                  start=k == 0, stop=k == KD - 1)
                last.then_inc(chunk_used, 1)
            arrived(pe, N_LATENT + 2)
            for t in range(TT):
                for k in range(KD):
                    last = mm(bank[4 + t // 2][:, t % 2 * 256:t % 2 * 256 + 256], hT[:, k, t * P:(t + 1) * P],
                              kview(N_LATENT + 2)[:, k, :], start=k == 0, stop=k == KD - 1)
            last.then_inc(chunk_used, 1)
            pe.drain().then_inc(step["latent_done"], 1)
            reached(pe, "latent_normed")
            for b in range(6):
                for t in range(TT):
                    src = cqn[:, t, b * P:(b + 1) * P] if b < 4 else ckvn[:, t, (b - 4) * P:(b - 3) * P]
                    last = pe.transpose(bank[b][:, t * P:(t + 1) * P], src, ident[:])
                last.then_inc(sem("latent_turned"), 1)
            reached(pe, "kr_ready")
            for t in range(TT):
                last = pe.transpose(bank[6][:, t * P:(t + 1) * P], kr_tok[:, t, :], ident[:])
            last.then_inc(step["kr_done"], 1)
            pe.wait_ge(sem("latent_T"), 6)
            reached(pe, "krT_ready")
            with pe.Fori(0, HEADS // 2) as i:
                pe.wait_ge(sem("mla_free"), i + 1)
                pe.wait_ge(sem("mla_w_in"), i * 32 + 32)
                for a in range(2):
                    for k in range(4):
                        last = mm(bank[a][:], mla_wq[:, k, a * QK:a * QK + NOPE], cqT[:, k, :], start=k == 0, stop=k == 3)
                    last.then_inc(sem("qk_done"), 1)
                for a in range(2):
                    for k in range(2):
                        last = mm(bank[3 + a][:], mla_wkv[:, k, a * 256:a * 256 + NOPE], ckvT[:, k, :], start=k == 0, stop=k == 1)
                    last.then_inc(sem("qk_done"), 1)
                w_rope = mla_wq[:].rearrange("p k (a n) -> p k a n", a=2)
                for t in range(TT):
                    for k in range(4):
                        last = mm(bank[2][:, t * P:(t + 1) * P].rearrange("p (a n) -> p a n", a=2), cqT[:, k, t * P:(t + 1) * P],
                                  w_rope[:, k, :, NOPE:QK], start=k == 0, stop=k == 3)
                last.then_inc(once_a_turn["qr_done"], 1)
                w_v = mla_wkv[:].rearrange("p k (a n) -> p k a n", a=2)
                for t in range(TT):
                    for k in range(2):
                        last = mm(bank[5 + t // 2][:, t % 2 * 256:t % 2 * 256 + 256].rearrange("p (a n) -> p a n", a=2),
                                  ckvT[:, k, t * P:(t + 1) * P], w_v[:, k, :, NOPE:NOPE + VD], start=k == 0, stop=k == 1)
                last.then_inc(once_a_turn["mla_w_used"], 1)
                pe.drain().then_inc(once_a_turn["v_mla_done"], 1)
                in_turn(pe, "qr_ready", i)
                for t in range(TT):
                    last = pe.transpose(bank[7][:, t * P:(t + 1) * P], qr_tok[:, t].rearrange("p a n -> p (a n)"), ident[:])
                last.then_inc(once_a_turn["qr_turned"], 1)
                pe.wait_ge(sem("qk_ready"), i * 4 + 4)
                in_turn(pe, "qrT_ready", i)
                in_turn(pe, "v_mla_ready", i)

                def scores(n):
                    a, q = n // 4, n % 4
                    if n >= 4:
                        pe.wait_ge(sem("exp_done"), i * 8 + n - 3)
                    mm(bank[n % 4][:], qT[:, a, q * P:(q + 1) * P], kT[:, a, :], start=True, stop=False)
                    rs = slice(a * 64, a * 64 + 64)
                    mm(bank[n % 4][:], qrT[rs, q * P:(q + 1) * P], krT[rs, :], start=False, stop=True).then_inc(sem("sc_done"), 1)

                def turn(n):
                    pe.wait_ge(sem("p_ready"), i * 8 + n + 1)
                    if n >= 2:
                        pe.wait_ge(sem("pT_ready"), i * 8 + n - 1)
                    for k in range(TT):
                        last = pe.transpose(bank[4 + n % 2][:, k * P:(k + 1) * P], probs[:, n % 2, k * P:(k + 1) * P], ident[:])
                    last.then_inc(sem("p_turned"), 1)

                def values(a):
                    pe.wait_ge(sem("pT_ready"), i * 8 + 4 * a + 4)
                    for k in range(TT):
                        last = mm(bank[6 + a][:], v_mla[:, k, a * VD:(a + 1) * VD], pT[:, a, k, :], start=k == 0, stop=k == TT - 1)
                    last.then_inc(sem("pv_done"), 1)

                scores(0)
                scores(1)
                for n in range(8):
                    if n + 2 < 8:
                        scores(n + 2)
                    if n == 5:
                        values(0)
                    turn(n)
                values(1)

            def mod_rows(n, dst):
                arrived(pe, n)
                for k in range(KD):
                    last = mm(dst, silu_cb[:, k, :], kview(n)[:, k, :], start=k == 0, stop=k == KD - 1)
                last.then_inc(chunk_used, 1)

            reached(pe, "silu_cb_ready")
            for j in range(4):
                mod_rows(N_MOD2 + j, bank[j // 2][:, j % 2 * 256:j % 2 * 256 + 256])
            for j in range(8):
                mod_cols(N_MOD2 + 4 + j, bank[2][:, 2 * j:2 * j + 2])
            for j in range(4):
                mod_rows(N_MOD2 + 12 + j, bank[3 + j // 2][:, j % 2 * 256:j % 2 * 256 + 256])
            pe.drain().then_inc(step["mod2_done"], 1)
            reached(pe, "mod2_cols")

            with pe.Fori(0, 2) as half:
                for c in range(2):
                    n = N_MERGE + 4 * c
                    for j, src in enumerate((hT, oT_dn, hT, oT_mla)):
                        arrived(pe, n + j, half, 8)
                        for b in range(2):
                            if j == 0:
                                pe.wait_ge(sem("sig_free"), half * 4 + c * 2 + b + 1)
                            for k in range(KD):
                                last = mm(bank[b * 4 + j][:], kview(n + j)[:, k, b * P:(b + 1) * P], src[:, k, :],
                                          start=k == 0, stop=k == KD - 1)
                            if j in (0, 2):
                                last.then_inc(sem("merge_done"), 1)
                            else:
                                last.then_inc(sem("branch_done"), 1)
                        pe.drain().then_inc(chunk_used, 1)

            pe.wait_ge(sem("sig_free"), 2 + 8)
            for c in range(4):
                arrived(pe, N_OUT + c)
                for t in range(TT):
                    if c >= 2:
                        pe.wait_ge(sem("out_added"), (c - 2) * TT + t + 1)
                    for k in range(KD):
                        last = mm(bank[c % 2 * 4 + t][:, 0:256], mT[:, k, t * P:(t + 1) * P], kview(N_OUT + c)[:, k, :],
                                  start=k == 0, stop=k == KD - 1)
                    last.then_inc(sem("out_done"), 1)
                pe.drain().then_inc(chunk_used, 1)

            norm_turn(1)
            normed(1)
            pe.wait_ge(sem("w_router_in"), 16)
            for t in range(TT):
                for k in range(KD):
                    last = mm(bank[0][:, t * 16:(t + 1) * 16], hT[:, k, t * P:(t + 1) * P], w_router[:, k, :],
                              start=k == 0, stop=k == KD - 1)
            last.then_inc(step["router_done"], 1)
            reached(pe, "aff_ready")
            for t in range(TT):
                last = pe.transpose(bank[1][0:EXPERTS, t * P:(t + 1) * P], aff[:, t, :], ident[:])
            last.then_inc(step["aff_turned"], 1)
            reached(pe, "slotT_ready")
            for t in range(TT):
                last = pe.transpose(bank[4][:, t * 16:(t + 1) * 16], slotT[:, t * P:(t + 1) * P], ident[0:EXPERTS, 0:EXPERTS])
            last.then_inc(step["slot_turned"], 1)
            reached(pe, "route_consts")
            for g in range(PAIRS):
                if g >= 2:
                    pe.wait_ge(sem("scat_ready"), g - 1)
                mm(bank[2 * (g % 2)][:], pair_sel[:, g, :], slotT[:], start=True, stop=True)
                mm(bank[2 * (g % 2) + 1][:], pair_sel[:, g, :], affT[:], start=True, stop=True).then_inc(sem("scat_rows"), 1)

            def gather(pair):
                for k in range(KD):
                    for t in range(TT):
                        sel = onehot[:, t, pair * P:(pair + 1) * P] if isinstance(pair, int) else onehot[:, t, bass.ds(pair * P, P)]
                        last = mm(bank[4 + k // 4][:, k % 4 * P:(k % 4 + 1) * P], xn[:, t, k * P:(k + 1) * P], sel,
                                  start=t == 0, stop=t == TT - 1)
                last.then_inc(sem("gather_done"), 1)

            reached(pe, "onehot_ready")
            gather(0)
            pe.wait_ge(sem("scat_ready"), PAIRS)
            with pe.Fori(0, PAIRS) as pair:
                def chunk_pair(n, first, lhs, banks, j):
                    for a in range(2):
                        arrived(pe, n + a, pair, PER_PAIR)
                    for kk in range(2):
                        for hf in range(2):
                            for a in range(2):
                                last = mm(bank[banks + hf][a * 64:a * 64 + 64, :], lhs[:, 2 * j + kk, a * 64:a * 64 + 64],
                                          wide(n + a)[:, kk, hf * 512:(hf + 1) * 512], start=2 * j + kk == 0, stop=2 * j + kk == 7)
                                if kk == 1 and hf == 1:
                                    last.then_inc(chunk_used, 1)

                n = N_EXPERT
                pe.wait_ge(sem("xeT_act"), pair + 1)
                pe.wait_ge(sem("xeT_dve"), pair + 1)
                for j in range(4):
                    chunk_pair(n + 2 * j, j == 0, xeT, 0, j)
                pe.drain().then_inc(once_a_turn["gate_done"], 1)
                for j in range(4):
                    chunk_pair(n + 8 + 2 * j, j == 0, xeT, 2, j)
                pe.drain().then_inc(once_a_turn["up_done"], 1)
                gather(pair + 1)
                pe.wait_ge(sem("hid_ready"), pair * 2 + 2)
                for k in range(KD):
                    last = pe.transpose(bank[k // 4][:, k % 4 * P:(k % 4 + 1) * P], hid[:, k * P:(k + 1) * P], ident[:])
                    if k % 4 == 3:
                        last.then_inc(sem("hid_turned"), 1)
                pe.wait_ge(sem("hidT_act"), pair + 1)
                pe.wait_ge(sem("hidT_dve"), pair + 1)
                for j in range(4):
                    chunk_pair(n + 16 + 2 * j, j == 0, hidT, 6, j)
                pe.drain().then_inc(once_a_turn["down_done"], 1)
            pe.wait_ge(sem("ye_act"), PAIRS)
            pe.wait_ge(sem("ye_dve"), PAIRS)
            pe.wait_ge(sem("xeT_act"), PAIRS + 1)
            pe.wait_ge(sem("xeT_dve"), PAIRS + 1)
            for t in range(TT):
                for hf in range(2):
                    for g in range(PAIRS):
                        last = mm(bank[2 * t + hf][:], scat[:, g, t * P:(t + 1) * P], ye[:, g, hf * 512:(hf + 1) * 512],
                                  start=g == 0, stop=g == PAIRS - 1)
                    last.then_inc(sem("scattered"), 1)

            reached(pe, "block2_consts")

            def mm3(dst, a, b, start, stop):
                mm(dst, a[0], b[0], start=start, stop=False)
                mm(dst, a[0], b[1], start=False, stop=False)
                return mm(dst, a[1], b[0], start=False, stop=stop)

            def both(ap, *idx):
                return [part[idx] for part in ap]

            h2T, y2T, hidT2 = (hT_hi, hT_lo), (yT_hi, yT_lo), (ffn_hi, ffn_lo)
            every = slice(None)

            def blocks2(dst, m, b):
                w = [split_k(part, m) for part in (w_hi, w_lo)]
                for k in range(KD):
                    last = mm3(dst, both(w, every, k, slice(b * P, (b + 1) * P)), both(h2T, every, k), k == 0, k == KD - 1)
                return last

            def tokens2(dst, t, src, m):
                w = [split_k(part, m) for part in (w_hi, w_lo)]
                for k in range(KD):
                    last = mm3(dst, both(src, every, k, slice(t * P, (t + 1) * P)), both(w, every, k), k == 0, k == KD - 1)
                return last

            pe.drain()
            pe.sem_inc(parts_used, 2)
            with pe.Fori(0, LAYERS) as l:
                m = M_IN
                pe.wait_ge(sem("x_ready"), l * 2 + 2)
                pe.wait_ge(sem("rows_l_in"), l * 208 + 208)
                pe.transpose(bank[0][:, 0:L_ROWS], rows_l[:], ident[0:L_ROWS, 0:L_ROWS]).then_inc(once_a_turn["rows_l_turned"], 1)
                norm_turn(l * 2 + 2, l * 2)
                pe.wait_ge(sem("hT_lo_ready"), l * (2 * KD) + KD)
                in_turn(pe, "cols_l_ready", l)
                for j, b0 in enumerate((0, 2, 4, 6, 0)):
                    parts_ready(pe, m, l)
                    if j == 4:
                        pe.wait_ge(sem("glu_ready"), l * 2 + 2)
                    for b in range(2):
                        blocks2(bank[b0 + b][:], m, b).then_inc(sem("proj_done"), 1)
                    pe.drain().then_inc(parts_used, 1)
                    m += 1
                for j, b0 in enumerate((4, 0, 4)):
                    if j == 0:
                        pe.wait_ge(sem("prod_ready"), l * 2 + 2)
                    if j == 1:
                        pe.wait_ge(sem("ya_ready"), l * 2 + 2)
                        pe.wait_ge(sem("glu_ready"), l * 2 + 2)
                    if j == 2:
                        for b in range(4):
                            pe.wait_ge(sem("rot_ready"), l * 8 + 4)
                            for t in range(TT):
                                last = pe.transpose(bank[4 + b][:, t * P:(t + 1) * P], rot[t // 2][:, t % 2, b * P:(b + 1) * P], ident[:])
                            last.then_inc(sem("qk2_turned"), 1)
                        pe.wait_ge(sem("qk2T_ready"), l * 8 + 4)
                    for c in range(2):
                        parts_ready(pe, m, l)
                        for t in range(TT):
                            last = tokens2(bank[b0 + t][:, c * 256:(c + 1) * 256], t, h2T, m)
                        last.then_inc(parts_used, 1)
                        m += 1
                    pe.drain().then_inc(once_a_turn[("q2_done", "k2_done", "v2_done")[j]], 1)
                pe.wait_ge(sem("rot_ready"), l * 8 + 8)
                for b in range(4):
                    for t in range(TT):
                        last = pe.transpose(bank[b][:, t * P:(t + 1) * P], rot[2 + t // 2][:, t % 2, b * P:(b + 1) * P], ident[:])
                    last.then_inc(sem("qk2_turned"), 1)
                pe.wait_ge(sem("qk2T_ready"), l * 8 + 8)
                in_turn(pe, "v2_ready", l)

                def scores2(i):
                    hd, q = i // 4, i % 4
                    if i >= 2:
                        pe.wait_ge(sem("exp2_done"), l * 32 + 2 * (i - 2) + 2)
                    rs = slice(hd % 2 * 64, hd % 2 * 64 + 64)
                    for m in range(2):
                        b = m * 2 + hd // 2
                        mm(bank[i % 2 * 2 + m][:, 0:(q + 1) * P], q2T[rs, b, q * P:(q + 1) * P], k2T[rs, b, 0:(q + 1) * P],
                           start=True, stop=True).then_inc(sem("sc2_done"), 1)

                def turn2(i):
                    pe.wait_ge(sem("a_ready"), l * 16 + i + 1)
                    if i >= 2:
                        pe.wait_ge(sem("aT_ready"), l * 16 + i - 1)
                    for k in range(i % 4 + 1):
                        last = pe.transpose(bank[4 + i % 2][:, k * P:(k + 1) * P], p2[:, i % 2 * 2, k * P:(k + 1) * P], ident[:])
                    last.then_inc(sem("a_turned"), 1)

                def values2(i):
                    hd, q = i // 4, i % 4
                    pe.wait_ge(sem("aT_ready"), l * 16 + i + 1)
                    if i >= 2:
                        pe.wait_ge(sem("o2_ready"), l * 16 + i - 1)
                    for k in range(q + 1):
                        last = mm(bank[6 + i % 2][:, 0:P], aT[:, i % 2, k, :], v2[:, k, hd * VD:(hd + 1) * VD], start=k == 0, stop=k == q)
                    last.then_inc(sem("pv2_done"), 1)

                scores2(0)
                for i in range(16):
                    if i + 1 < 16:
                        scores2(i + 1)
                    turn2(i)
                    if i >= 1:
                        values2(i - 1)
                values2(15)
                pe.wait_ge(sem("conf_ready"), l * 2 + 2)
                pe.wait_ge(sem("exp2_done"), l * 32 + 32)
                for b in range(2):
                    last = mm(bank[0][:], ones[:], conf[:, b, :], start=b == 0, stop=b == 1)
                last.then_inc(once_a_turn["conf_mean"], 1)
                pe.wait_ge(sem("conf_sq"), l * 2 + 2)
                for b in range(2):
                    last = mm(bank[1][:], ones[:], conv_acc[:, b, :], start=b == 0, stop=b == 1)
                last.then_inc(once_a_turn["conf_var"], 1)
                in_turn(pe, "o2_normed", l)
                for b in range(4):
                    for t in range(TT):
                        last = pe.transpose(bank[4 + b][:, t * P:(t + 1) * P], o2[:, t, b, :], ident[:])
                    last.then_inc(sem("o2_turned"), 1)
                pe.wait_ge(sem("yT_lo_ready"), l * KD + KD)
                for c in range(4):
                    parts_ready(pe, m, l)
                    for t in range(TT):
                        if c >= 2:
                            pe.wait_ge(sem("out2_added"), l * 16 + (c - 2) * TT + t + 1)
                        tokens2(bank[c % 2 * 4 + t][:, 0:256], t, y2T, m).then_inc(sem("out2_done"), 1)
                    pe.drain().then_inc(parts_used, 1)
                    m += 1
                norm_turn(l * 2 + 3, l * 2 + 1)
                pe.wait_ge(sem("hT_lo_ready"), l * (2 * KD) + 2 * KD)
                for j in range(FB // 2):
                    for s in range(2):
                        parts_ready(pe, m, l)
                        for b in range(2):
                            if j >= 2 and s == 0:
                                pe.wait_ge(sem("ffn_hid"), l * FB + 2 * (j - 2) + b + 1)
                            last = blocks2(bank[j % 2 * 4 + 2 * s + b][:], m, b)
                            last.then_inc(sem("ffn_up" if s else "ffn_gate"), 1)
                        pe.drain().then_inc(parts_used, 1)
                        m += 1
                pe.wait_ge(sem("ffn_hid"), l * FB + FB)
                for j in range(FB // 2):
                    parts_ready(pe, m, l)
                    pe.wait_ge(sem("ffn_lo_ready"), l * (FB // 2) + j + 1)
                    w = [split_wide(part, m) for part in (w_hi, w_lo)]
                    for t in range(TT):
                        for hf in range(2):
                            for b in range(2):
                                last = mm3(bank[2 * t + hf][:], both(hidT2, every, j % 2, b, slice(t * P, (t + 1) * P)),
                                           both(w, every, b, slice(hf * 512, (hf + 1) * 512)), j + b == 0, j + b == FB // 2)
                    last.then_inc(parts_used, 1)
                    m += 1
                pe.drain().then_inc(once_a_turn["ffn_done"], 1)

        @block.vector
        def _(dve):
            ts, tt, stt = dve.tensor_scalar, dve.tensor_tensor, dve.scalar_tensor_tensor
            copy = dve.tensor_copy

            dve.memset(eps_col[:, 0:1], EPS)
            dve.memset(eps_col[:, 1:2], LN_EPS)
            dve.drain().then_inc(step["eps_ready"], 1)
            reached(dve, "rows_turned")
            copy(cols_a[:], bank[6][:, 0:R_A])
            copy(cols_b[:], bank[7][:, 0:CONV_K * 24])
            dve.drain().then_inc(step["cols_ready"], 1)
            dve.wait_ge(sem("aux_in"), 80)
            copy(pos_f[:], pos_i[:])
            dve.drain()
            for t in range(8):
                ts(ang[:, t, :], inv_freq[:], pos_f[:, t:t + 1], None, ALU.mult)
            dve.drain()
            for dst, quarter in ((sin, 0.0), (cos, float(np.pi / 2))):
                ts(turns[:], ang[:], quarter, float(1 / (2 * np.pi)), ALU.add, ALU.mult)
                dve.drain()
                ts(turns[:], turns[:], MAGIC, None, ALU.add)
                dve.drain()
                ts(turns[:], turns[:], -MAGIC, None, ALU.add)
                dve.drain()
                stt(dst[:], turns[:], -TWO_PI_HI, ang[:], ALU.mult, ALU.add)
                dve.drain()
                stt(dst[:], turns[:], -TWO_PI_MID, dst[:], ALU.mult, ALU.add)
                dve.drain()
                stt(dst[:], turns[:], -TWO_PI_LO, dst[:], ALU.mult, ALU.add)
                dve.drain()
                ts(dst[:], dst[:], quarter, PI_IN, ALU.add, ALU.min)
                dve.drain()
                ts(dst[:], dst[:], -PI_IN, None, ALU.max)
                dve.drain()
            dve.drain().then_inc(step["angles_ready"], 1)
            reached(dve, "masks_ready")
            for d in range(2):
                ts(min_mask[:, d, :], tri[:, d, :], -1.0, BIG, ALU.add, ALU.mult)
                tt(max_mask[:, d, :], ident[:], tri[:, 1 - d, :], ALU.subtract)
            dve.drain()
            for d in range(2):
                ts(max_mask[:, d, :], max_mask[:, d, :], 1.0, BIG, ALU.add, ALU.mult)

            def norm_scale(n, gain, shift):
                dve.wait_ge(sem("rms_ready"), n + 1)
                dve.reciprocal(rstd[:, 0:TT], rms[:, 0:TT])
                dve.drain()
                for t in range(TT):
                    ts(xn[:, t, :], x[:, t, :], rstd[:, t:t + 1], None, ALU.mult)
                dve.drain().then_inc(sem("xn_ready"), 1)
                if gain is None:
                    return
                norm_turned(n, gain, shift)

            def norm_turned(n, gain, shift):
                for k in range(0, KD, 2):
                    dve.wait_ge(sem("turned"), n * KD + k + 1)
                    if shift is None:
                        last = ts(hT[:, k, :], bank[4 + k % 4][:], gain(k), None, ALU.mult)
                    else:
                        last = ts(hT[:, k, :], bank[4 + k % 4][:], gain(k), shift(k), ALU.mult, ALU.add)
                    last.then_inc(sem("hT_dve"), 1)

            reached(dve, "mod1_done")
            tt(mod_sh1[:], bank[0][:, 0:8], cols_a[:, R_BMOD:R_BMOD + 8], ALU.add)
            tt(mod_g1[:], bank[0][:, 8:16], cols_a[:, R_BMOD + 8:R_BMOD + 16], ALU.add)
            dve.drain()
            stt(mod_g1[:], mod_g1[:], 1.0, cols_a[:, R_GMIX:R_GMIX + 8], ALU.add, ALU.mult)
            dve.drain().then_inc(step["mod1_cols"], 1)
            norm_scale(0, lambda k: mod_g1[:, k:k + 1], lambda k: mod_sh1[:, k:k + 1])

            reached(dve, "small_ready")
            tt(sp_a[:], small[:, :, 16:32], dt_b[:].unsqueeze(1).to_broadcast([P, TT, 16]), ALU.add)
            dve.drain()
            stt(sp_b[:], sp_a[:], -1.0, sp_a[:], ALU.mult, ALU.max)
            dve.drain().then_inc(step["sp_in"], 1)
            reached(dve, "sp_ready")
            stt(sp_a[:], sp_a[:], 0.0, sp_b[:], ALU.max, ALU.add)
            dve.drain()
            g = col_q[:, 4].rearrange("p (t d) h -> p t (d h)", t=TT)
            stt(g, sp_a[:], -1.0, a_log_b[:].unsqueeze(1).to_broadcast([P, TT, 16]), ALU.mult, ALU.mult)
            dve.drain().then_inc(step["g_ready"], 1)
            reached(dve, "gc_done")
            copy(col_q[:, 1].rearrange("p a h -> p (a h)"), bank[1][:, 0:64])
            dve.drain()
            tt(col_q[:, 3].rearrange("p a h -> p (a h)"), bank[2][:, 0:64], col_q[:, 1].rearrange("p a h -> p (a h)"), ALU.subtract)
            dve.drain().then_inc(step["gc_ready"], 1)
            reached(dve, "gc_exp")
            tt(col_q[:, 2], col_q[:, 2], col_q[:, 0], ALU.mult)
            dve.drain()

            reached(dve, "rope_ready")
            with dve.Fori(0, HEADS) as h:
                dve.wait_ge(sem("head_done"), h + 1)
                copy(head_q[:].unsqueeze(3), col_q[:, :, :, bass.ds(h, 1)])
                copy(conv_col[:].unsqueeze(3), cols_b[:].rearrange("p (j s h) -> p j s h", j=CONV_K, s=3)[:, :, :, bass.ds(h, 1)])
                dve.drain().then_inc(once_a_turn["head_q_ready"], 1)
                copy(g_wide[:].rearrange("p t d n -> p (t d) n"), head_q[:, 4, :].unsqueeze(2).to_broadcast([P, TT * 2, P]))\
                    .then_inc(once_a_turn["g_wide_ready"], 1)
                for s in range(3):
                    dve.wait_ge(sem("qkv_done"), h * 3 + s + 1)
                    ts(conv_out[:, s, :], bank[s][:], conv_col[:, 2, s:s + 1], None, ALU.mult)
                    for j in (0, 1, 3, 4):
                        o = j - 2
                        lo, hi = max(0, -o), SEQ - max(0, o)
                        dve.drain()
                        last = stt(conv_out[:, s, lo:hi], bank[s][:, lo + o:hi + o], conv_col[:, j, s:s + 1],
                                   conv_out[:, s, lo:hi], ALU.mult, ALU.add)
                    last.then_inc(sem("conv_done"), 1)
                in_turn(dve, "len_ready", h)
                dve.reciprocal(rstd[:, 0:8], rms[:, 0:8])
                dve.drain()
                for t in range(TT):
                    ts(q_tok[:, t, :], bank[4][:, t * P:(t + 1) * P], rstd[:, t:t + 1], float(HD) ** -0.5, ALU.mult, ALU.mult)
                dve.drain().then_inc(once_a_turn["q_tok_ready"], 1)
                for t in range(TT):
                    ts(k_tok[:, t, :], bank[5][:, t * P:(t + 1) * P], rstd[:, 4 + t:5 + t], None, ALU.mult)
                dve.drain().then_inc(once_a_turn["k_tok_ready"], 1)
                for d in range(2):
                    dve.wait_ge(sem("e_row_ready"), h * 2 + d + 1)
                    row = bank[7 if d == 0 else 2]
                    for t in range(TT):
                        col = head_q[:, 1, 2 * t + d:2 * t + d + 1]
                        stt(e_T[:, d, t, :], row[:, t * P:(t + 1) * P], col, min_mask[:, d, :], ALU.subtract, ALU.min)
                        last = stt(e_L[:, d, t, :], row[:, t * P:(t + 1) * P], col, max_mask[:, d, :], ALU.subtract, ALU.max)
                    last.then_inc(sem("e_arg_ready"), 1)
                in_turn(dve, "kk_done", h)
                for d in range(2):
                    dve.wait_ge(sem("e_ready"), h * 2 + d + 1)
                    for t in range(TT):
                        last = stt(e_L[:, d, t, :], bank[3][:, t * P:(t + 1) * P], head_q[:, 0, 2 * t + d:2 * t + d + 1],
                                   e_L[:, d, t, :], ALU.mult, ALU.mult)
                    last.then_inc(sem("L_ready"), 1)
                in_turn(dve, "kq_done", h)
                for d in range(2):
                    et = e_T[:, d].rearrange("p t n -> p (t n)")
                    tt(et, bank[6][:], et, ALU.mult)
                for d in range(2):
                    last = tt(q_decT[:, d, :], qnT[:], e_row[:, d, :], ALU.mult)
                    dve.drain().then_inc(sem("q_dec_ready"), 1)
                eye = ident[:].unsqueeze(1).to_broadcast([P, TT, P])
                for d in range(2):
                    dve.wait_ge(sem("C_ready"), h * 12 + d + 1)
                    tt(solve_T[:, d, :].rearrange("p (t n) -> p t n", t=TT), eye, solve_C[:, d], ALU.subtract)
                    dve.wait_ge(sem("n_done"), h * 12 + d + 1)
                    tt(solve_TT[:, d, :].rearrange("p (t n) -> p t n", t=TT), eye,
                       bank[d][:].rearrange("p (t n) -> p t n", t=TT), ALU.subtract)
                    dve.drain().then_inc(sem("T_ready"), 1)
                for lv in range(1, 6):
                    for d in range(2):
                        dve.wait_ge(sem("dTT_done"), h * 10 + 2 * (lv - 1) + d + 1)
                        tt(solve_TT[:, d, :], solve_TT[:, d, :], bank[7 if d == 0 else 2][:], ALU.subtract)
                        if lv < 5:
                            dve.wait_ge(sem("dT_done"), h * 8 + 2 * (lv - 1) + d + 1)
                            tt(solve_T[:, d, :], solve_T[:, d, :], bank[4 + d][:], ALU.subtract)
                        dve.drain().then_inc(sem("T_ready"), 1)
                for d in range(2):
                    last = dve.memset(state[:, d, :], 0.0)
                    last.then_inc(sem("state_ready"), 1)
                dve.wait_ge(sem("u_ready"), h * 2 + 2)
                for s in range(8):
                    for d in range(2):
                        c = s if d == 0 else 7 - s
                        t, r0 = c // 2, c % 2 * 64
                        rs = slice(r0, r0 + 64)
                        dve.wait_ge(sem("ws_done"), h * 16 + 2 * s + d + 1)
                        tt(v_new[rs, d, :], u[rs, d, t, :], bank[d][rs, 0:P], ALU.subtract).then_inc(sem("v_new_ready"), 1)
                    if s < 7:
                        for d in range(2):
                            c = s if d == 0 else 7 - s
                            end = c * 64 + (63 if d == 0 else 0)
                            dve.wait_ge(sem("ds_done"), h * 14 + 2 * s + d + 1)
                            stt(state[:, d, :], state[:, d, :], e_row[:, d, end:end + 1], bank[4 + d][:, 0:P], ALU.mult, ALU.add)\
                                .then_inc(sem("state_ready"), 1)
                in_turn(dve, "o_fwd_ready", h)
                dve.wait_ge(sem("o_done"), h * 2 + 2)
                of = o_tok[:].rearrange("p t n -> p (t n)")
                tt(of, of, bank[2][:], ALU.add).then_inc(once_a_turn["o_sum"], 1)
                in_turn(dve, "o_rms", h)
                dve.reciprocal(rstd[:, 0:TT], rms[:, 0:TT])
                dve.drain()
                for t in range(TT):
                    stt(o_tok[:, t, :], o_tok[:, t, :], rstd[:, t:t + 1], z_silu[:, t, :], ALU.mult, ALU.mult)
                dve.drain().then_inc(once_a_turn["o_ready"], 1)

            reached(dve, "latent_rms")
            dve.reciprocal(rstd[:, 0:8], rms[:, 0:8])
            dve.drain()
            for t in range(TT):
                ts(cqn[:, t, :], bank[t][:], rstd[:, t:t + 1], None, ALU.mult)
                ts(ckvn[:, t, :], bank[4 + t // 2][:, t % 2 * 256:t % 2 * 256 + 256], rstd[:, 4 + t:5 + t], None, ALU.mult)
            dve.drain().then_inc(step["latent_normed"], 1)

            def rotate(lo, hi, c, s, src_lo, src_hi):
                shape = list(src_lo.shape)
                n = int(np.prod(shape[1:]))
                fit = {3: "p (a b) -> p a b", 4: "p (a b c) -> p a b c"}[len(shape)]
                sizes = dict(zip("abc", shape[1:]))
                t0 = rope_buf[:, 0, 0:n].rearrange(fit, **sizes)
                t1 = rope_buf[:, 1, 0:n].rearrange(fit, **sizes)
                tt(t0, src_lo, c, ALU.mult)
                tt(t1, src_hi, s, ALU.mult)
                dve.drain()
                tt(lo, t0, t1, ALU.subtract)
                dve.drain()
                tt(t0, src_hi, c, ALU.mult)
                tt(t1, src_lo, s, ALU.mult)
                dve.drain()
                tt(hi, t0, t1, ALU.add)
                dve.drain()

            rope_buf = rope_t
            for a in range(2):
                rotate(kr_tok[:, :, a * 64:a * 64 + 32], kr_tok[:, :, a * 64 + 32:a * 64 + 64], cos[:, 0:TT, :], sin[:, 0:TT, :],
                       small[:, :, 32:64], small[:, :, 64:96])
            dve.drain().then_inc(step["kr_ready"], 1)
            with dve.Fori(0, HEADS // 2) as i:
                dve.wait_ge(sem("mla_free"), i + 1)
                in_turn(dve, "qr_done", i)
                qr = bank[2][:].rearrange("p (t a n) -> p t a n", t=TT, a=2)
                c4 = cos[:, 0:TT, :].unsqueeze(2).to_broadcast([P, TT, 2, 32])
                s4 = sin[:, 0:TT, :].unsqueeze(2).to_broadcast([P, TT, 2, 32])
                rotate(qr_tok[:, :, :, 0:32], qr_tok[:, :, :, 32:64], c4, s4, qr[:, :, :, 0:32], qr[:, :, :, 32:64])
                dve.drain().then_inc(once_a_turn["qr_ready"], 1)
                in_turn(dve, "v_mla_done", i)
                for b in range(2):
                    copy(v_mla[:, 2 * b:2 * b + 2, :].rearrange("p t n -> p (t n)"), bank[5 + b][:])
                dve.drain().then_inc(once_a_turn["v_mla_ready"], 1)
                in_turn(dve, "qr_turned", i)
                copy(qrT[:], bank[7][:]).then_inc(once_a_turn["qrT_ready"], 1)

                def row_max(n):
                    dve.wait_ge(sem("sc_done"), i * 8 + n + 1)
                    dve.tensor_reduce(nmax[:, n % 2:n % 2 + 1], bank[n % 4][:], AX_X, ALU.max)
                    dve.drain()
                    ts(nmax[:, n % 2:n % 2 + 1], nmax[:, n % 2:n % 2 + 1], -float(QK) ** -0.5, None, ALU.mult).then_inc(sem("nmax_ready"), 1)

                row_max(0)
                for n in range(8):
                    if n + 1 < 8:
                        row_max(n + 1)
                    dve.wait_ge(sem("exp_done"), i * 8 + n + 1)
                    dve.reciprocal(pinv[:, n % 2:n % 2 + 1], psums[:, n % 2:n % 2 + 1])
                    dve.drain()
                    ts(probs[:, n % 2, :], probs[:, n % 2, :], pinv[:, n % 2:n % 2 + 1], None, ALU.mult).then_inc(sem("p_ready"), 1)

            dve.wait_ge(sem("mla_free"), 1 + HEADS // 2)
            copy(silu_cb[:], silu_c[:].unsqueeze(2).to_broadcast([P, KD, P]))
            dve.drain().then_inc(step["silu_cb_ready"], 1)
            reached(dve, "mod2_done")
            dve.wait_ge(sem("gt1_in"), 16)
            dve.wait_ge(sem("gt2_in"), 16)
            for hf in range(2):
                c = slice(hf * 512, hf * 512 + 512)
                tt(gt1_b[:, c], gt1_b[:, c], bank[hf][:], ALU.add)
                tt(gt2_b[:, c], gt2_b[:, c], bank[3 + hf][:], ALU.add)
            tt(mod_sh2[:], bank[2][:, 0:8], cols_a[:, R_BMOD + 24:R_BMOD + 32], ALU.add)
            tt(mod_g2[:], bank[2][:, 8:16], cols_a[:, R_BMOD + 32:R_BMOD + 40], ALU.add)
            dve.drain()
            stt(mod_g2[:], mod_g2[:], 1.0, cols_a[:, R_GFFN:R_GFFN + 8], ALU.add, ALU.mult)
            dve.drain().then_inc(step["mod2_cols"], 1)

            dve.sem_inc(sem("sig_free"), 2)
            with dve.Fori(0, 2) as half:
                for c in range(2):
                    for b in range(2):
                        for j in range(2):
                            dve.wait_ge(sem("branch_done"), half * 8 + c * 4 + j * 2 + b + 1)
                            dve.wait_ge(sem("sig_ready"), half * 8 + c * 4 + j * 2 + b + 1)
                            tt(part[:, b, j, :], sig[:, b, j, :], bank[b * 4 + 2 * j + 1][:], ALU.mult)
                        dve.drain()
                        tt(mT[:, bass.ds(half * 4 + (c * 2 + b), 1), :].rearrange("p a n -> p (a n)"), part[:, b, 0, :], part[:, b, 1, :], ALU.add)
                        dve.drain().then_inc(sem("sig_free"), 1)

            for c in range(4):
                for t in range(TT):
                    dve.wait_ge(sem("out_done"), c * TT + t + 1)
                    cs = slice(c * 256, c * 256 + 256)
                    tt(upd[:], bank[c % 2 * 4 + t][:, 0:256], gt1_b[:, cs], ALU.mult)
                    dve.drain()
                    tt(x[:, t, cs], x[:, t, cs], upd[:], ALU.add)
                    dve.drain().then_inc(sem("out_added"), 1)
            dve.drain().then_inc(sem("x_ready"), 1)

            norm_scale(1, lambda k: mod_g2[:, k:k + 1], lambda k: mod_sh2[:, k:k + 1])
            reached(dve, "router_done")
            dve.tensor_reduce(amax[:], bank[0][:, 0:TT * 16].rearrange("p (t e) -> p t e", t=TT), AX_X, ALU.max)
            dve.drain()
            ts(amax[:], amax[:], -1.0, None, ALU.mult)
            dve.drain().then_inc(step["amax_ready"], 1)
            reached(dve, "aff_exp")
            dve.reciprocal(asum[:], asum[:])
            dve.drain()
            tt(aff[:], aff[:], asum[:].unsqueeze(2).to_broadcast([P, TT, EXPERTS]), ALU.mult)
            dve.drain().then_inc(step["aff_ready"], 1)
            reached(dve, "aff_turned")
            copy(affT[:], bank[1][0:EXPERTS, :])
            copy(work[:, 0, :], bank[1][0:EXPERTS, :])
            dve.drain()
            for i in range(CAP // 8):
                dve.max(top8[:, i, :], work[:, i % 2, :])
                dve.drain()
                dve.match_replace(work[:, 1 - i % 2, :], top8[:, i, :], work[:, i % 2, :], -1.0)
                dve.drain()
            ts(work[:, 0, :], work[:, 0, :], 0.0, None, ALU.is_lt)
            reached(dve, "route_consts")
            dve.drain()
            dve.tensor_tensor_scan(work[:, 1, :], work[:, 0, :], zeros16[:], 0.0, ALU.add, ALU.add)
            dve.drain()
            tt(work[:, 1, :], work[:, 1, :], work[:, 0, :], ALU.mult)
            dve.drain()
            ts(slotT[:], work[:, 1, :], -1.0, None, ALU.add)
            dve.drain().then_inc(step["slotT_ready"], 1)
            reached(dve, "slot_turned")
            copy(slot_tok[:].rearrange("p t e -> p (t e)"), bank[4][:, 0:TT * 16])
            dve.drain()
            for t in range(TT):
                tt(onehot[:, t, 0:PAIRS * P].rearrange("p (e s) -> p e s", e=EXPERTS),
                   slot_tok[:, t, :].unsqueeze(2).to_broadcast([P, EXPERTS, 64]),
                   iota64[:].unsqueeze(1).to_broadcast([P, EXPERTS, 64]), ALU.is_equal)
            dve.drain().then_inc(step["onehot_ready"], 1)
            for g in range(PAIRS):
                dve.wait_ge(sem("gate_b_ready"), g + 1)
                stt(scat[:, g, :], bank[2 * (g % 2)][:], iota_p[:], gate_b[:, g % 2, :], ALU.is_equal, ALU.mult)\
                    .then_inc(sem("scat_ready"), 1)

            def gathered(n):
                dve.wait_ge(sem("gather_done"), n)
                for k in range(4):
                    last = ts(xeT[:, k, :], bank[4][:, k * P:(k + 1) * P], mod_g2[:, k:k + 1], mod_sh2[:, k:k + 1], ALU.mult, ALU.add)
                last.then_inc(sem("xeT_dve"), 1)

            gathered(1)
            with dve.Fori(0, PAIRS) as pair:
                in_turn(dve, "up_done", pair)
                for hf in range(2):
                    dve.wait_ge(sem("silu_hid"), pair * 2 + hf + 1)
                    c = slice(hf * 512, hf * 512 + 512)
                    tt(hid[:, c], hid[:, c], bank[2 + hf][:], ALU.mult).then_inc(sem("hid_ready"), 1)
                gathered(pair + 2)
                dve.wait_ge(sem("hid_turned"), pair * 2 + 2)
                copy(hidT[:, 4:8, :].rearrange("p k n -> p (k n)"), bank[1][:]).then_inc(sem("hidT_dve"), 1)
                in_turn(dve, "down_done", pair)
                copy(ye[:, bass.ds(pair, 1), 512:1024].rearrange("p a n -> p (a n)"), bank[7][:]).then_inc(sem("ye_dve"), 1)
            for t in range(TT):
                for hf in range(2):
                    dve.wait_ge(sem("scattered"), 2 * t + hf + 1)
                    c = slice(hf * 512, hf * 512 + 512)
                    tt(upd2[:], bank[2 * t + hf][:], gt2_b[:, c], ALU.mult)
                    dve.drain()
                    tt(x[:, t, c], x[:, t, c], upd2[:], ALU.add)
                    dve.drain()
            dve.drain().then_inc(step["x_first"], 1)
            reached(dve, "first_rms")
            dve.wait_ge(sem("gfin_in"), 32)
            dve.reciprocal(rstd[:, 0:TT], rms[:, 0:TT])
            dve.drain()
            for t in range(TT):
                stt(x[:, t, :], x[:, t, :], rstd[:, t:t + 1], gfin_b[:], ALU.mult, ALU.mult)
            dve.memset(glu[:, :, 0:30], 0.0)
            dve.memset(prod[:, :, 0:2], 0.0)
            dve.drain()
            dve.drain().then_inc(sem("x_ready"), 1)

            for l in range(LAYERS):
                lam_init = 0.8 - 0.6 * float(np.exp(-0.3 * l))
                dve.memset(lam_c[:, l, 0:1], lam_init)
                dve.memset(lam_c[:, l, 1:2], 1.0 - lam_init)
            reached(dve, "block2_consts")
            dve.drain()
            rope_buf = rope_2

            def turned_lo(n, gain):
                for k in range(KD):
                    dve.wait_ge(sem("hT_hi_ready"), n * KD + k + 1)
                    stt(hT_lo[:, k, :], bank[4 + k % 4][:], gain(k), hT_hi[:, k, :].bitcast(F32), ALU.mult, ALU.subtract)\
                        .then_inc(sem("hT_lo_ready"), 1)

            with dve.Fori(0, LAYERS) as l:
                in_turn(dve, "rows_l_turned", l)
                copy(cols_l[:], bank[0][:, 0:L_ROWS])
                dve.drain().then_inc(once_a_turn["cols_l_ready"], 1)
                dve.sem_inc(sem("rows_l_free"), 1)
                dve.memset(glu[:, :, 0:30], 0.0)
                dve.memset(prod[:, :, 0:2], 0.0)
                dve.wait_ge(sem("rows_l_in"), l * 208 + 208)
                for j in range(2):
                    tt(lam_p[:, j, :], lam_in[:, 2 * j, :], lam_in[:, 2 * j + 1, :], ALU.mult)
                dve.drain()
                dve.tensor_reduce(lam_s[:, 0:2], lam_p[:], AX_X, ALU.add)
                dve.drain().then_inc(once_a_turn["lam_dots"], 1)
                norm_scale(l * 2 + 2, None, None)
                turned_lo(l * 2, lambda k: cols_l[:, L_MIX + k:L_MIX + k + 1])
                in_turn(dve, "lam_exp", l)
                copy(lam_s[:, 2:4].unsqueeze(1), lam_c[:, bass.ds(l, 1), :])
                tt(lam_i[:, 0:1], lam_s[:, 0:1], lam_s[:, 1:2], ALU.subtract)
                dve.drain()
                tt(lam_i[:, 0:1], lam_i[:, 0:1], lam_s[:, 2:3], ALU.add)
                tt(lam_i[:, 1:2], cols_l[:, L_SUB:L_SUB + 1], lam_s[:, 3:4], ALU.mult)
                dve.drain()
                for b in range(2):
                    dve.wait_ge(sem("glu_sig"), l * 2 + b + 1)
                    stt(glu[:, b, 30:], bank[b][:], cols_l[:, L_GLU + b:L_GLU + b + 1], sig2[:, b, :], ALU.add, ALU.mult)\
                        .then_inc(sem("glu_ready"), 1)
                for b in range(2):
                    dve.wait_ge(sem("ac_ready"), l * 2 + b + 1)
                    dve.wait_ge(sem("proj_done"), l * 10 + 7 + b)
                    tt(prod[:, b, 2:], prod[:, b, 2:], bank[6 + b][:], ALU.mult).then_inc(sem("prod_ready"), 1)
                dve.drain()
                for b in range(2):
                    w = lambda j: cols_l[:, L_SC + 2 * j + b:L_SC + 2 * j + b + 1]
                    ya = conv_acc[:, b, :]
                    ts(ya, prod[:, b, 0:SEQ], w(0), None, ALU.mult)
                    for j in (1, 2):
                        dve.drain()
                        stt(ya, prod[:, b, j:j + SEQ], w(j), ya, ALU.mult, ALU.add)
                    dve.drain()
                    dve.wait_ge(sem("proj_done"), l * 10 + 9 + b)
                    tt(ya, ya, bank[b][:], ALU.mult).then_inc(sem("ya_ready"), 1)
                    dve.drain()
                    copy(yT_hi[:, b, :], ya)
                c3 = lambda tb: tb.unsqueeze(1).to_broadcast([P, 8, 32])
                for j in range(2):
                    in_turn(dve, "k2_done" if j else "q2_done", l)
                    for t in range(TT):
                        src = bank[(0 if j else 4) + t][:].rearrange("p (g n) -> p g n", g=8)
                        dst = rot[2 * j + t // 2][:, t % 2, :].rearrange("p (g n) -> p g n", g=8)
                        rotate(dst[:, :, 0:32], dst[:, :, 32:64], c3(cos[:, TT + t, :]), c3(sin[:, TT + t, :]), src[:, :, 0:32], src[:, :, 32:64])
                        dve.drain().then_inc(sem("rot_ready"), 1)

                def long_conv(first, last_tap):
                    for j in range(first, last_tap):
                        for b in range(2):
                            w = cols_l[:, L_DW + 2 * j + b:L_DW + 2 * j + b + 1]
                            if j == 0:
                                ts(conf[:, b, :], glu[:, b, 0:SEQ], w, cols_l[:, L_DWB + b:L_DWB + b + 1], ALU.mult, ALU.add)
                            else:
                                stt(conf[:, b, :], glu[:, b, j:j + SEQ], w, conf[:, b, :], ALU.mult, ALU.add)
                        dve.drain()

                def row_max2(n):
                    w = (n % 4 + 1) * P
                    for m in range(2):
                        j = n % 2 * 2 + m
                        dve.wait_ge(sem("sc2_done"), l * 32 + 2 * n + m + 1)
                        tt(bank[j][:, w - P:w], bank[j][:, w - P:w], causal[:], ALU.add)
                        dve.drain()
                        dve.tensor_reduce(nmax2[:, j:j + 1], bank[j][:, 0:w], AX_X, ALU.max)
                        dve.drain()
                        ts(nmax2[:, j:j + 1], nmax2[:, j:j + 1], -0.125, None, ALU.mult).then_inc(sem("nmax2_ready"), 1)

                def combine(n):
                    w, j = (n % 4 + 1) * P, n % 2 * 2
                    dve.wait_ge(sem("exp2_done"), l * 32 + 2 * n + 2)
                    dve.reciprocal(pinv2[:, j:j + 2], psum2[:, j:j + 2])
                    dve.drain()
                    ts(p2[:, j + 1, 0:w], p2[:, j + 1, 0:w], pinv2[:, j + 1:j + 2], lam_i[:, 0:1], ALU.mult, ALU.mult)
                    dve.drain()
                    stt(p2[:, j, 0:w], p2[:, j, 0:w], pinv2[:, j:j + 1], p2[:, j + 1, 0:w], ALU.mult, ALU.subtract).then_inc(sem("a_ready"), 1)

                in_turn(dve, "v2_done", l)
                for b in range(2):
                    tt(yT_lo[:, b, :], conv_acc[:, b, :], yT_hi[:, b, :].bitcast(F32), ALU.subtract).then_inc(sem("yT_lo_ready"), 1)
                row_max2(0)
                for n in range(16):
                    if n + 1 < 16:
                        row_max2(n + 1)
                    combine(n)
                    long_conv(2 * n, min(2 * n + 2, CONF_K))
                for b in range(2):
                    dve.drain().then_inc(sem("conf_ready"), 1)
                in_turn(dve, "o2_rms", l)
                dve.reciprocal(rstd[:], rms[:])
                dve.drain()
                for n in range(16):
                    ts(o2[:, n % 4, n // 4, :], o2[:, n % 4, n // 4, :], rstd[:, n:n + 1], None, ALU.mult)
                dve.drain().then_inc(once_a_turn["o2_normed"], 1)
                in_turn(dve, "conf_mean", l)
                for b in range(2):
                    stt(conf[:, b, :], bank[0][:], -1.0 / 256, conf[:, b, :], ALU.mult, ALU.add).then_inc(sem("conf_centred"), 1)
                in_turn(dve, "ln_rms", l)
                dve.reciprocal(ln_rs[:], ln_rs[:])
                dve.drain()
                for b in range(2):
                    tt(conf[:, b, :], conf[:, b, :], ln_rs[:], ALU.mult).then_inc(sem("conf_normed"), 1)
                for b in range(6):
                    dve.wait_ge(sem("yT_hi_ready"), l * 6 + b + 1)
                    if b < 4:
                        last = stt(yT_lo[:, 2 + b, :], bank[4 + b][:], lam_i[:, 1:2], yT_hi[:, 2 + b, :].bitcast(F32), ALU.mult, ALU.subtract)
                    else:
                        last = tt(yT_lo[:, 2 + b, :], conv_acc[:, b - 4, :], yT_hi[:, 2 + b, :].bitcast(F32), ALU.subtract)
                    last.then_inc(sem("yT_lo_ready"), 1)
                for c in range(4):
                    for t in range(TT):
                        dve.wait_ge(sem("out2_done"), l * 16 + c * TT + t + 1)
                        cs = slice(c * 256, c * 256 + 256)
                        tt(x[:, t, cs], x[:, t, cs], bank[c % 2 * 4 + t][:, 0:256], ALU.add).then_inc(sem("out2_added"), 1)
                dve.drain().then_inc(sem("x_ready"), 1)
                norm_scale(l * 2 + 3, None, None)
                turned_lo(l * 2 + 1, lambda k: cols_l[:, L_FFN + k:L_FFN + k + 1])

                def hid_lo(j):
                    dve.wait_ge(sem("ffn_hi_ready"), l * (FB // 2) + j + 1)
                    tt(ffn_lo[:, j % 2], ffn_hT[:, 2 * j:2 * j + 2, :], ffn_hi[:, j % 2].bitcast(F32), ALU.subtract)\
                        .then_inc(sem("ffn_lo_ready"), 1)

                for f in range(FB):
                    dve.wait_ge(sem("ffn_up"), l * FB + f + 1)
                    dve.wait_ge(sem("ffn_silu"), l * FB + f + 1)
                    tt(ffn_hT[:, f, :], ffn_sg[:, f % 4, :], bank[(f // 2 % 2) * 4 + 2 + f % 2][:], ALU.mult).then_inc(sem("ffn_hid"), 1)
                for j in range(FB // 2):
                    hid_lo(j)
                in_turn(dve, "ffn_done", l)
                for t in range(TT):
                    for hf in range(2):
                        c = slice(hf * 512, hf * 512 + 512)
                        tt(x[:, t, c], x[:, t, c], bank[2 * t + hf][:], ALU.add)
                dve.drain().then_inc(sem("x_ready"), 1)
            reached(dve, "last_rms")
            dve.reciprocal(rstd[:, 0:TT], rms[:, 0:TT])
            dve.drain()
            for t in range(TT):
                stt(x[:, t, :], x[:, t, :], rstd[:, t:t + 1], gfin2_b[:], ALU.mult, ALU.mult).then_inc(sem("y_ready"), 1)


_INS = ['x', 'c', 'positions', 'w_mod', 'b_mod', 'g_mix', 'w_in', 'conv_w', 'a_log', 'dt_bias', 'dn_o_gain', 'q_gain', 'w_uq',
        'kv_gain', 'w_ukv', 'w_o_dn', 'w_o_mla', 'w_out', 'g_ffn', 'w_router', 'w_gate', 'w_up', 'w_down', 'g_final',
        'positions_2', 'mix_norm_g_2', 'w_in_2', 'short_conv_w_2', 'glu_b_2', 'conf_dw_w_2', 'conf_dw_b_2', 'conf_ln_g_2',
        'conf_ln_b_2', 'lam_q1_2', 'lam_k1_2', 'lam_q2_2', 'lam_k2_2', 'diff_subln_g_2', 'w_out_2', 'ffn_norm_g_2',
        'w_gate_2', 'w_up_2', 'w_down_2', 'final_norm_g_2']


def kernel(**inputs):
    import numpy as _np
    import concourse.bacc as _bacc
    from concourse import mybir as _mybir
    from concourse.bass_utils import run_bass_kernel_spmd as _run

    nc = _bacc.Bacc("TRN2", target_bir_lowering=False, num_devices=1)
    arrays, args = {}, {}
    for name in _INS:
        arrays[name] = _np.ascontiguousarray(inputs[name])
    arrays["inv_freq"] = _np.power(_np.float32(10000.0), -_np.arange(32, dtype=_np.float32) / _np.float32(32)).reshape(1, 32)
    for name, a in arrays.items():
        args[name] = nc.dram_tensor(f"in_{name}", a.shape, _mybir.dt.from_np(a.dtype), kind="ExternalInput").ap()
    out = nc.dram_tensor("out", (1, SEQ, DM), _mybir.dt.float32, kind="ExternalOutput").ap()
    build(nc, args, out)
    r = _run(nc, [{f"in_{k}": v for k, v in arrays.items()}], core_ids=[0])
    return r.results[0]["out"]
```
